# Optimizing a Trainium2 kernel written in Bass

```python
import math
import jax
import jax.numpy as jnp
from jax import lax
import numpy as np

D_MODEL = 1024
BATCH = 1
SEQ = 128
DEPTH = 2
DEC_BATCH = 1
DEC_SEQ = 128
PAST_LEN = 128

GRID_W = 64
HEAD_DIM = 64
N_MOD = 6
RMS_EPS = 1e-6
N_ATTN_LAYERS = (DEPTH + 1) // 2
N_REC_LAYERS = DEPTH // 2
A_HEADS = D_MODEL // (2 * HEAD_DIM)
A_KV_HEADS = A_HEADS // 4
WINDOW = 128
ROPE_BASE = 10000.0
QBLK = 128
B_HEADS = D_MODEL // (2 * HEAD_DIM)
NA_ROWS = 8
NA_COLS = 16
C_DIM = D_MODEL // 2
C_SHORT = 3
C_EMB = 33
C_FFN = 64
HYENA_MIN_DECAY = math.log(1e-2) / 1.5
HYENA_MAX_DECAY = math.log(1e-2) / 0.3
D_KDIM = 128
D_VDIM = 128
D_HEADS = (D_MODEL // 2) // D_VDIM
D_CHUNK = 32
N_EXPERTS = 64
TOP_K = 8
D_EXPERT = 256
D_SHARED = 256
ROUTE_SCALE = 2.5
MOE_BLK = 128

A_Q = A_HEADS * HEAD_DIM
A_KV = A_KV_HEADS * HEAD_DIM
B_W = B_HEADS * HEAD_DIM
ATTN_SPLITS = (A_Q, A_KV, A_KV, B_W, B_W, B_W)
ATTN_IN = A_Q + 2 * A_KV + 3 * B_W
D_KTOT = D_HEADS * D_KDIM
D_VTOT = D_HEADS * D_VDIM
REC_SPLITS = (3 * C_DIM, D_KTOT, D_KTOT, D_KTOT, D_VTOT, D_VTOT)
REC_IN = 3 * C_DIM + 3 * D_KTOT + 2 * D_VTOT

kernel_name = 'hybrid_diffusion_prefix_trunk'

def rmsnorm(x, g):
    xf = x.astype(jnp.float32)
    y = xf * lax.rsqrt(jnp.mean(xf * xf, axis=-1, keepdims=True) + RMS_EPS)
    return (y * g.astype(jnp.float32)).astype(x.dtype)

def modulate(h, shift, scale):
    return h * (1 + scale) + shift

def adaln(cvec, w, b):
    m = jax.nn.silu(cvec) @ w + b
    return jnp.split(m[:, None, :], N_MOD, axis=-1)

def split_cols(x, sizes):
    out, start = [], 0
    for s in sizes:
        out.append(x[..., start:start + s])
        start += s
    return out

def axial_rope(x):
    L, Dh = x.shape[1], x.shape[-1]
    half = Dh // 2
    t = jnp.arange(L)
    inv = ROPE_BASE ** (-jnp.arange(0, half, 2, dtype=jnp.float32) / half)

    def rot(xa, pos):
        ang = pos.astype(jnp.float32)[:, None] * inv[None, :]
        cos = jnp.cos(ang)[None, :, None, :].astype(x.dtype)
        sin = jnp.sin(ang)[None, :, None, :].astype(x.dtype)
        x1, x2 = xa[..., :half // 2], xa[..., half // 2:]
        return jnp.concatenate([x1 * cos - x2 * sin, x1 * sin + x2 * cos], axis=-1)

    return jnp.concatenate([rot(x[..., :half], t // GRID_W), rot(x[..., half:], t % GRID_W)], axis=-1)

def context_attention(q, k, v, sink):
    B, L, HK, G, Dh = q.shape
    nb = L // QBLK
    scale = Dh ** -0.5
    qb = jnp.moveaxis(q.reshape(B, nb, QBLK, HK, G, Dh), 1, 0)

    def block(qi):
        s = jnp.einsum('bqhgd,bkhd->bhgqk', qi, k).astype(jnp.float32) * scale
        if sink is not None:
            sk = jnp.broadcast_to(sink.astype(jnp.float32)[None, :, :, None, None], s.shape[:-1] + (1,))
            s = jnp.concatenate([s, sk], axis=-1)
        p = jax.nn.softmax(s, axis=-1)[..., :L]
        return jnp.einsum('bhgqk,bkhd->bqhgd', p.astype(v.dtype), v)

    o = lax.map(block, qb)
    return jnp.moveaxis(o, 0, 1).reshape(B, L, HK * G * Dh)

def window_attention(q_raw, q_rot, k_rot, v, k_ctx, v_ctx, sink):
    B, L, HQ, Dh = q_rot.shape
    HK = k_rot.shape[2]
    G = HQ // HK
    Lc = k_ctx.shape[1]
    nb = L // WINDOW
    scale = Dh ** -0.5

    def blocks(t):
        return t.reshape(B, nb, WINDOW, HK, G, Dh)

    def band(t):
        tp = jnp.pad(t, ((0, 0), (WINDOW, WINDOW), (0, 0), (0, 0))).reshape(B, nb + 2, WINDOW, HK, Dh)
        return jnp.concatenate([tp[:, :-2], tp[:, 1:-1], tp[:, 2:]], axis=2)

    kb, vb = band(k_rot), band(v)
    s_loc = jnp.einsum('bnqhgd,bnkhd->bnhgqk', blocks(q_rot), kb).astype(jnp.float32) * scale
    qi = jnp.arange(WINDOW)
    kj = jnp.arange(3 * WINDOW)
    rel = kj[None, :] - WINDOW - qi[:, None]
    kpos = (jnp.arange(nb)[:, None] - 1) * WINDOW + kj[None, :]
    valid = (jnp.abs(rel) <= WINDOW)[None] & ((kpos >= 0) & (kpos < L))[:, None, :]
    s_loc = jnp.where(valid[None, :, None, None], s_loc, -jnp.inf)
    s_ctx = jnp.einsum('bnqhgd,bchd->bnhgqc', blocks(q_raw), k_ctx).astype(jnp.float32) * scale
    s_sink = jnp.broadcast_to(sink.reshape(HK, G).astype(jnp.float32)[None, None, :, :, None, None], s_loc.shape[:-1] + (1,))
    p = jax.nn.softmax(jnp.concatenate([s_ctx, s_loc, s_sink], axis=-1), axis=-1)
    o = (jnp.einsum('bnhgqc,bchd->bnqhgd', p[..., :Lc].astype(v.dtype), v_ctx)
         + jnp.einsum('bnhgqk,bnkhd->bnqhgd', p[..., Lc:Lc + 3 * WINDOW].astype(v.dtype), vb))
    return o.reshape(B, L, HQ * Dh)

def neighborhood_attention(q, k, v, k_ctx, v_ctx, rpb):
    B, L, H, Dh = q.shape
    Lc = k_ctx.shape[1]
    rows = L // GRID_W
    wr = min(NA_ROWS, rows)
    scale = Dh ** -0.5
    r = jnp.arange(rows)
    rs = jnp.clip(r - NA_ROWS // 2, 0, rows - wr)
    band_rows = rs[:, None] + jnp.arange(wr)[None, :]

    def gather(t):
        return t.reshape(B, rows, GRID_W, H, Dh)[:, band_rows].reshape(B, rows, wr * GRID_W, H, Dh)

    kg, vg = gather(k), gather(v)
    qg = q.reshape(B, rows, GRID_W, H, Dh)
    s_loc = jnp.einsum('brqhd,brkhd->bhrqk', qg, kg).astype(jnp.float32) * scale
    cq = jnp.arange(GRID_W)
    cs = jnp.clip(cq - NA_COLS // 2, 0, GRID_W - NA_COLS)
    col_ok = (cq[None, :] >= cs[:, None]) & (cq[None, :] < cs[:, None] + NA_COLS)
    mask = jnp.broadcast_to(col_ok[:, None, :], (GRID_W, wr, GRID_W)).reshape(GRID_W, wr * GRID_W)
    idx_r = band_rows - r[:, None] + NA_ROWS - 1
    idx_c = jnp.clip(cq[None, :] - cq[:, None], -(NA_COLS - 1), NA_COLS - 1) + NA_COLS - 1
    bias = rpb[:, idx_r[:, None, :, None], idx_c[None, :, None, :]]
    bias = bias.reshape(H, rows, GRID_W, wr * GRID_W).astype(jnp.float32)
    s_loc = jnp.where(mask, s_loc + bias, -jnp.inf)
    s_ctx = jnp.einsum('brqhd,bchd->bhrqc', qg, k_ctx).astype(jnp.float32) * scale
    p = jax.nn.softmax(jnp.concatenate([s_ctx, s_loc], axis=-1), axis=-1)
    o = (jnp.einsum('bhrqc,bchd->brqhd', p[..., :Lc].astype(v.dtype), v_ctx)
         + jnp.einsum('bhrqk,brkhd->brqhd', p[..., Lc:].astype(v.dtype), vg))
    return o.reshape(B, L, H * Dh)

def attn_mixer_context(h, w_in, w_out, sink):
    B, L, _ = h.shape
    G = A_HEADS // A_KV_HEADS
    q_a, k_a, v_a, q_b, k_b, v_b = split_cols(h @ w_in, ATTN_SPLITS)
    k_a = k_a.reshape(B, L, A_KV_HEADS, HEAD_DIM)
    v_a = v_a.reshape(B, L, A_KV_HEADS, HEAD_DIM)
    k_b = k_b.reshape(B, L, B_HEADS, HEAD_DIM)
    v_b = v_b.reshape(B, L, B_HEADS, HEAD_DIM)
    o_a = context_attention(q_a.reshape(B, L, A_KV_HEADS, G, HEAD_DIM), k_a, v_a, sink.reshape(A_KV_HEADS, G))
    o_b = context_attention(q_b.reshape(B, L, B_HEADS, 1, HEAD_DIM), k_b, v_b, None)
    out = jnp.concatenate([o_a, o_b], axis=-1) @ w_out
    return out, k_a, v_a, k_b, v_b

def attn_mixer_latent(h, ck_a, cv_a, ck_b, cv_b, w_in, w_out, sink, rpb):
    B, L, _ = h.shape
    q_a, k_a, v_a, q_b, k_b, v_b = split_cols(h @ w_in, ATTN_SPLITS)
    q_a = q_a.reshape(B, L, A_HEADS, HEAD_DIM)
    k_a = k_a.reshape(B, L, A_KV_HEADS, HEAD_DIM)
    v_a = v_a.reshape(B, L, A_KV_HEADS, HEAD_DIM)
    o_a = window_attention(q_a, axial_rope(q_a), axial_rope(k_a), v_a, ck_a, cv_a, sink)
    hb = lambda t: t.reshape(B, L, B_HEADS, HEAD_DIM)
    o_b = neighborhood_attention(hb(q_b), hb(k_b), hb(v_b), ck_b, cv_b, rpb)
    return jnp.concatenate([o_a, o_b], axis=-1) @ w_out

def hyena_filter(L, w1, b1, w2, b2, w3, b3, freq, w4):
    f32 = jnp.float32
    t = jnp.linspace(0.0, 1.0, L, dtype=f32)[:, None]
    bands = (C_EMB - 1) // 2
    ang = (2.0 * math.pi / L) * jnp.arange(L, dtype=f32)[:, None] * jnp.linspace(1e-4, bands - 1, bands, dtype=f32)[None, :]
    z = jnp.concatenate([t, jnp.cos(ang), -jnp.sin(ang)], axis=-1)
    fr = freq.astype(f32)
    act = lambda y: jnp.sin(fr * y)
    hh = act(z @ w1.astype(f32) + b1.astype(f32))
    hh = act(hh @ w2.astype(f32) + b2.astype(f32))
    hh = act(hh @ w3.astype(f32) + b3.astype(f32))
    hh = hh @ w4.astype(f32)
    deltas = jnp.abs(jnp.linspace(HYENA_MIN_DECAY, HYENA_MAX_DECAY, C_DIM, dtype=f32))
    window = jnp.exp(-t * deltas[None, :])
    return hh.reshape(L, 2, C_DIM) * window[:, None, :]

def hyena(u, conv_w, conv_b, filt, d_skip):
    B, L, C3 = u.shape
    u = lax.conv_general_dilated(u, conv_w[:, None, :].astype(u.dtype), (1,), [((C_SHORT - 1) // 2, (C_SHORT - 1) // 2)],
                                 dimension_numbers=('NWC', 'WIO', 'NWC'), feature_group_count=C3) + conv_b.astype(u.dtype)
    x0, x1, v = u[..., :C_DIM], u[..., C_DIM:2 * C_DIM], u[..., 2 * C_DIM:]
    z = (x1 * v).astype(jnp.float32)
    h = hyena_filter(L, *filt)
    n = 2 * L
    zf = jnp.fft.rfft(z, n=n, axis=1)
    hf = jnp.fft.rfft(h[:, 0], n=n, axis=0) + jnp.conj(jnp.fft.rfft(h[:, 1], n=n, axis=0))
    y = jnp.fft.irfft(zf * hf[None], n=n, axis=1)[:, :L]
    y = y + z * d_skip.astype(jnp.float32)
    return (x0.astype(jnp.float32) * y).astype(u.dtype)

def gla_chunked(q, k, v, log_f, s0):
    B, L, H, DK = q.shape
    DV = v.shape[-1]
    nc = L // D_CHUNK

    def chunks(t):
        return t.reshape(B, nc, D_CHUNK, H, t.shape[-1]).transpose(1, 0, 3, 2, 4)

    qc, kc, vc, gc = chunks(q), chunks(k), chunks(v), chunks(log_f)
    b = jnp.cumsum(gc, axis=3)
    causal = jnp.tril(jnp.ones((D_CHUNK, D_CHUNK), dtype=bool))
    rel = jnp.where(causal[:, :, None], b[..., :, None, :] - b[..., None, :, :], -jnp.inf)
    scores = jnp.einsum('nbhtk,nbhsk,nbhtsk->nbhts', qc, kc, jnp.exp(rel))
    o_intra = jnp.einsum('nbhts,nbhsv->nbhtv', scores, vc)
    q_in = qc * jnp.exp(b)
    k_out = kc * jnp.exp(b[..., -1:, :] - b)
    decay = jnp.exp(b[..., -1, :])

    def step(S, inp):
        qi, ki, vi, di = inp
        o = jnp.einsum('bhtk,bhkv->bhtv', qi, S)
        S = di[..., None] * S + jnp.einsum('bhtk,bhtv->bhkv', ki, vi)
        return S, o

    s_fin, o_inter = lax.scan(step, s0, (q_in, k_out, vc, decay))
    o = (o_intra + o_inter).transpose(1, 0, 3, 2, 4).reshape(B, L, H, DV)
    return o, s_fin

def lower_bound(gamma, layer):
    p = jax.nn.softmax(gamma.astype(jnp.float32), axis=0)
    return (jnp.cumsum(p, axis=0) - p[0])[layer]

def hgrn2(q, f_fwd, f_bwd, i, g, s0_f, s0_b, lb_f, lb_b, norm_g):
    B, L, _ = q.shape
    f32 = jnp.float32
    heads = lambda t, d: t.reshape(B, L, D_HEADS, d)
    qh = heads(jax.nn.silu(q.astype(f32)), D_KDIM)
    vh = heads(i.astype(f32), D_VDIM)

    def gates(fx, lb):
        f = lb + (1.0 - lb) * jax.nn.sigmoid(fx.astype(f32))
        return heads(1.0 - f, D_KDIM), heads(jnp.log(f), D_KDIM)

    kf, lff = gates(f_fwd, lb_f)
    kb, lfb = gates(f_bwd, lb_b)
    rev = lambda t: jnp.flip(t, axis=1)
    o_f, s_f = gla_chunked(qh, kf, vh, lff, s0_f.astype(f32))
    o_b, s_b = gla_chunked(rev(qh), rev(kb), rev(vh), rev(lfb), s0_b.astype(f32))
    o = rmsnorm(o_f + rev(o_b), norm_g).reshape(B, L, D_VTOT)
    o = o * jax.nn.silu(g.astype(f32))
    return o.astype(q.dtype), s_f.astype(q.dtype), s_b.astype(q.dtype)

def rec_mixer(h, s0_f, s0_b, lb_f, lb_b, w_in, w_out, conv_w, conv_b, filt, d_skip, norm_g):
    u_c, q_d, f_f, f_b, i_d, g_d = split_cols(h @ w_in, REC_SPLITS)
    y_c = hyena(u_c, conv_w, conv_b, filt, d_skip)
    o_d, s_f, s_b = hgrn2(q_d, f_f, f_b, i_d, g_d, s0_f, s0_b, lb_f, lb_b, norm_g)
    return jnp.concatenate([y_c, o_d], axis=-1) @ w_out, s_f, s_b

def moe(x, w_router, router_bias, w_gate, w_up, w_down, ws_gate, ws_up, ws_down):
    shp = x.shape
    xt = x.reshape(-1, shp[-1])
    T, D = xt.shape
    scores = jax.nn.sigmoid((xt @ w_router).astype(jnp.float32))
    _, idx = lax.top_k(scores + router_bias.astype(jnp.float32), TOP_K)
    gate = jnp.take_along_axis(scores, idx, axis=-1)
    gate = gate / jnp.sum(gate, axis=-1, keepdims=True) * ROUTE_SCALE
    A = T * TOP_K
    e_flat = idx.reshape(-1)
    tok = jnp.arange(A) // TOP_K
    order = jnp.argsort(e_flat)
    e_sorted, tok_sorted, g_sorted = e_flat[order], tok[order], gate.reshape(-1)[order]
    counts = jnp.bincount(e_flat, length=N_EXPERTS)
    padded = ((counts + MOE_BLK - 1) // MOE_BLK) * MOE_BLK
    pad_end = jnp.cumsum(padded)
    pad_start = pad_end - padded
    grp_start = jnp.cumsum(counts) - counts
    dest = pad_start[e_sorted] + jnp.arange(A) - grp_start[e_sorted]
    n_rows = ((A + N_EXPERTS * (MOE_BLK - 1) + MOE_BLK - 1) // MOE_BLK) * MOE_BLK
    nb = n_rows // MOE_BLK
    blk_expert = jnp.minimum(jnp.searchsorted(pad_end, jnp.arange(nb) * MOE_BLK, side='right'), N_EXPERTS - 1)
    buf = jnp.zeros((n_rows, D), xt.dtype).at[dest].set(xt[tok_sorted])

    def expert_block(args):
        xb, e = args
        hb = jax.nn.silu(xb @ w_gate[e]) * (xb @ w_up[e])
        return hb @ w_down[e]

    yb = lax.map(expert_block, (buf.reshape(nb, MOE_BLK, D), blk_expert)).reshape(n_rows, D)
    routed = jnp.zeros((T, D), jnp.float32).at[tok_sorted].add(g_sorted[:, None] * yb[dest].astype(jnp.float32))
    shared = (jax.nn.silu(xt @ ws_gate) * (xt @ ws_up)) @ ws_down
    return (routed + shared.astype(jnp.float32)).astype(x.dtype).reshape(shp)

def setup_inputs(seed: int = 0) -> dict:
    key = jax.random.key(seed)
    keys = iter(jax.random.split(key, 48))
    f32 = jnp.float32

    def nrm(shape, std):
        return jax.random.normal(next(keys), shape, f32) * std

    def gain(shape):
        return 1.0 + nrm(shape, 0.05)

    D = D_MODEL
    return {
        'x_prompt': nrm((BATCH, SEQ, D), 1.0),
        'x_sample': nrm((DEC_BATCH, DEC_SEQ, D), 1.0),
        'cache_a_k': nrm((DEC_BATCH, N_ATTN_LAYERS, PAST_LEN, A_KV_HEADS, HEAD_DIM), 1.0),
        'cache_a_v': nrm((DEC_BATCH, N_ATTN_LAYERS, PAST_LEN, A_KV_HEADS, HEAD_DIM), 1.0),
        'cache_b_k': nrm((DEC_BATCH, N_ATTN_LAYERS, PAST_LEN, B_HEADS, HEAD_DIM), 1.0),
        'cache_b_v': nrm((DEC_BATCH, N_ATTN_LAYERS, PAST_LEN, B_HEADS, HEAD_DIM), 1.0),
        'state_d_fwd': nrm((DEC_BATCH, N_REC_LAYERS, D_HEADS, D_KDIM, D_VDIM), 0.5),
        'state_d_bwd': nrm((DEC_BATCH, N_REC_LAYERS, D_HEADS, D_KDIM, D_VDIM), 0.5),
        'c': nrm((DEC_BATCH, D), 1.0),
        'c_ctx': nrm((D,), 1.0),
        'w_ada': nrm((DEPTH, D, N_MOD * D), 0.5 * D ** -0.5),
        'b_ada': nrm((DEPTH, N_MOD * D), 0.02),
        'norm_mix': gain((DEPTH, D)),
        'norm_ffn': gain((DEPTH, D)),
        'w_in_attn': nrm((N_ATTN_LAYERS, D, ATTN_IN), D ** -0.5),
        'w_out_attn': nrm((N_ATTN_LAYERS, A_Q + B_W, D), (A_Q + B_W) ** -0.5),
        'sink_a': nrm((N_ATTN_LAYERS, A_HEADS), 1.0),
        'rpb_b': nrm((N_ATTN_LAYERS, B_HEADS, 2 * NA_ROWS - 1, 2 * NA_COLS - 1), 0.1),
        'w_in_rec': nrm((N_REC_LAYERS, D, REC_IN), D ** -0.5),
        'w_out_rec': nrm((N_REC_LAYERS, C_DIM + D_VTOT, D), (C_DIM + D_VTOT) ** -0.5),
        'conv_w': nrm((N_REC_LAYERS, C_SHORT, 3 * C_DIM), C_SHORT ** -0.5),
        'conv_b': nrm((N_REC_LAYERS, 3 * C_DIM), 0.02),
        'filt_w1': nrm((N_REC_LAYERS, C_EMB, C_FFN), C_EMB ** -0.5),
        'filt_b1': nrm((N_REC_LAYERS, C_FFN), 0.1),
        'filt_w2': nrm((N_REC_LAYERS, C_FFN, C_FFN), C_FFN ** -0.5),
        'filt_b2': nrm((N_REC_LAYERS, C_FFN), 0.1),
        'filt_w3': nrm((N_REC_LAYERS, C_FFN, C_FFN), C_FFN ** -0.5),
        'filt_b3': nrm((N_REC_LAYERS, C_FFN), 0.1),
        'filt_freq': gain((N_REC_LAYERS, C_FFN)),
        'filt_w4': nrm((N_REC_LAYERS, C_FFN, 2 * C_DIM), 0.1 * C_FFN ** -0.5),
        'd_skip': nrm((N_REC_LAYERS, C_DIM), 1.0),
        'lb_fwd': nrm((DEPTH, D_KTOT), 0.1),
        'lb_bwd': nrm((DEPTH, D_KTOT), 0.1),
        'norm_d': gain((N_REC_LAYERS, D_VDIM)),
        'w_router': nrm((DEPTH, D, N_EXPERTS), D ** -0.5),
        'router_bias': nrm((DEPTH, N_EXPERTS), 0.01),
        'w_gate': nrm((DEPTH, N_EXPERTS, D, D_EXPERT), D ** -0.5),
        'w_up': nrm((DEPTH, N_EXPERTS, D, D_EXPERT), D ** -0.5),
        'w_down': nrm((DEPTH, N_EXPERTS, D_EXPERT, D), D_EXPERT ** -0.5),
        'ws_gate': nrm((DEPTH, D, D_SHARED), D ** -0.5),
        'ws_up': nrm((DEPTH, D, D_SHARED), D ** -0.5),
        'ws_down': nrm((DEPTH, D_SHARED, D), D_SHARED ** -0.5),
        'final_norm': gain((D,)),
    }

def reference(x_prompt, x_sample, cache_a_k, cache_a_v, cache_b_k, cache_b_v, state_d_fwd, state_d_bwd, c, c_ctx,
              w_ada, b_ada, norm_mix, norm_ffn, w_in_attn, w_out_attn, sink_a, rpb_b, w_in_rec, w_out_rec,
              conv_w, conv_b, filt_w1, filt_b1, filt_w2, filt_b2, filt_w3, filt_b3, filt_freq, filt_w4, d_skip,
              lb_fwd, lb_bwd, norm_d, w_router, router_bias, w_gate, w_up, w_down, ws_gate, ws_up, ws_down,
              final_norm):
    def filt(j):
        return (filt_w1[j], filt_b1[j], filt_w2[j], filt_b2[j], filt_w3[j], filt_b3[j], filt_freq[j], filt_w4[j])

    def ffn(l, t):
        return moe(t, w_router[l], router_bias[l], w_gate[l], w_up[l], w_down[l], ws_gate[l], ws_up[l], ws_down[l])

    def rec(l, h, s0_f, s0_b):
        j = l // 2
        return rec_mixer(h, s0_f, s0_b, lower_bound(lb_fwd, l), lower_bound(lb_bwd, l), w_in_rec[j], w_out_rec[j],
                         conv_w[j], conv_b[j], filt(j), d_skip[j], norm_d[j])

    xp = x_prompt
    ak, av, bk, bv, sf, sb = [], [], [], [], [], []
    for l in range(DEPTH):
        j = l // 2
        sh1, sc1, g1, sh2, sc2, g2 = adaln(c_ctx[None, :], w_ada[l], b_ada[l])
        h = modulate(rmsnorm(xp, norm_mix[l]), sh1, sc1)
        if l % 2 == 0:
            out, k_a, v_a, k_b, v_b = attn_mixer_context(h, w_in_attn[j], w_out_attn[j], sink_a[j])
            ak.append(k_a)
            av.append(v_a)
            bk.append(k_b)
            bv.append(v_b)
        else:
            s0 = jnp.zeros((xp.shape[0], D_HEADS, D_KDIM, D_VDIM), jnp.float32)
            out, s_f, s_b = rec(l, h, s0, s0)
            sf.append(s_f)
            sb.append(s_b)
        xp = xp + g1 * out
        xp = xp + g2 * ffn(l, modulate(rmsnorm(xp, norm_ffn[l]), sh2, sc2))
    y_prompt = rmsnorm(xp, final_norm)

    xs = x_sample
    for l in range(DEPTH):
        j = l // 2
        sh1, sc1, g1, sh2, sc2, g2 = adaln(c, w_ada[l], b_ada[l])
        h = modulate(rmsnorm(xs, norm_mix[l]), sh1, sc1)
        if l % 2 == 0:
            out = attn_mixer_latent(h, cache_a_k[:, j], cache_a_v[:, j], cache_b_k[:, j], cache_b_v[:, j],
                                    w_in_attn[j], w_out_attn[j], sink_a[j], rpb_b[j])
        else:
            out, _, _ = rec(l, h, state_d_fwd[:, j], state_d_bwd[:, j])
        xs = xs + g1 * out
        xs = xs + g2 * ffn(l, modulate(rmsnorm(xs, norm_ffn[l]), sh2, sc2))
    y_sample = rmsnorm(xs, final_norm)

    new_a_k = jnp.stack(ak, axis=1)
    new_a_v = jnp.stack(av, axis=1)
    new_b_k = jnp.stack(bk, axis=1)
    new_b_v = jnp.stack(bv, axis=1)
    new_d_fwd = jnp.stack(sf, axis=1)
    new_d_bwd = jnp.stack(sb, axis=1)
    return (y_prompt, y_sample, new_a_k, new_a_v, new_b_k, new_b_v, new_d_fwd, new_d_bwd)


_drawn_inputs = setup_inputs


def setup_inputs(seed=0):
    import zlib

    import numpy as np

    out = dict(_drawn_inputs(seed))
    spreads = {}
    factors = {'state_d_fwd': 8.0,
     'state_d_bwd': 7.168,
     'sink_a': 8.0,
     'rpb_b': 4.331,
     'conv_b': 3.245,
     'filt_b1': 3.266,
     'filt_b2': 2.723,
     'filt_freq': 4.415,
     'norm_d': 3.504}
    for name, (base, spread) in spreads.items():
        noise = np.random.default_rng([zlib.crc32(name.encode()), seed]).standard_normal(out[name].shape)
        drawn = base * np.exp(spread * noise) if base else spread * noise
        out[name] = jnp.asarray(drawn.astype(out[name].dtype))
    for name, factor in factors.items():
        out[name] = (out[name] * factor).astype(out[name].dtype)
    return out
```

```python
from contextlib import ExitStack
import math

import numpy as np
import concourse.bass as bass
from concourse import mybir

F32 = mybir.dt.float32
BF16 = mybir.dt.bfloat16
I32 = mybir.dt.int32
U8 = mybir.dt.uint8
U32 = mybir.dt.uint32
ALU = mybir.AluOpType
ACT = mybir.ActivationFunctionType
AX = mybir.AxisListType.X

P = 128
D = 1024
KC = D // P
G = 2
GROW = 32
N_MOD = 6
EPS = 1e-6
NE, FE = 64, 256
HD = 64
ATTN_IN, REC_IN = 2304, 4096
QA, KA, VA, QB, KB, VB = 0, 512, 640, 768, 1280, 1792
CQ, CF, CI, CG = 1536, 2048, 3072, 3584
GRID_W, NA_COLS = 64, 16
NHD = 4
LEVELS = [64, 32, 16, 8, 4, 2, 1]
MAGIC = 1.5 * 2.0 ** 23
TWO_PI = 2.0 * math.pi
PI_1, PI_2 = 6.28125, 0.0019350051879882812
PI_3 = TWO_PI - PI_1 - PI_2
BIG = 1e30
CAP = 96
NR = 8
NROW = G * P * NR
SKIP = NROW
U = 4


def constants():
    t = np.arange(P)
    out = {}
    out["ident"] = np.eye(P)

    def exponents(back):
        u, x = t[:, None], t[None, :]
        if back:
            u, x = P - 1 - u, P - 1 - x
        blocks = []
        for m in LEVELS:
            mid = (x // (2 * m)) * 2 * m + m
            blocks.append(np.where((x // m) % 2 == 1, (u >= mid) & (u <= x), (u > x) & (u < mid)))
        blocks.append(u <= x)
        return np.concatenate(blocks, axis=1)

    out["expo"] = np.concatenate([exponents(False), exponents(True)], axis=1)
    out["tail"] = np.concatenate([t[:, None] > t[None, :], t[:, None] < t[None, :]], axis=1)
    ang = 2 * np.pi * np.outer(t, t) / (2 * P)
    alt = (-1.0) ** t
    f_cos, f_sin0 = np.cos(ang), -np.sin(ang)
    f_sin, f_cosn = f_sin0.copy(), f_cos.copy()
    f_sin[:, 0] = alt
    f_cosn[:, 0] = alt
    f_sin0[:, 0] = 0
    i_cos, i_sin = np.cos(ang) / P, -np.sin(ang) / P
    i_cos[0] /= 2
    i_sin[0] = alt / (2 * P)
    out["dft"] = np.concatenate([f_cos, f_sin, f_sin0, f_cosn, i_cos, i_sin], axis=1)
    lin = np.linspace(0.0, 1.0, P, dtype=np.float32).astype(np.float64)
    lo, hi = math.log(1e-2) / 1.5, math.log(1e-2) / 0.3
    out["window"] = np.exp(-lin[:, None] * np.abs(np.linspace(lo, hi, 512))[None, :])
    bands = 16
    a2 = (2 * np.pi / P) * t[:, None] * np.linspace(1e-4, bands - 1, bands)[None, :]
    z = np.zeros((P, P))
    z[:33] = np.concatenate([lin[:, None], np.cos(a2), -np.sin(a2)], axis=1).T
    out["zemb"] = z
    inv = 10000.0 ** (-np.arange(0, 32, 2) / 32)
    pos = np.stack([t // GRID_W, t % GRID_W], axis=1)
    ra = (pos[:, :, None] * inv[None, None, :]).reshape(P, 32)
    out["rope"] = np.concatenate([np.cos(ra), np.sin(ra)], axis=1)
    col = t % GRID_W
    cs = np.clip(col - NA_COLS // 2, 0, GRID_W - NA_COLS)
    ok = (col[None, :] >= cs[:, None]) & (col[None, :] < cs[:, None] + NA_COLS)
    out["namask"] = np.where(ok, 0.0, -BIG)
    out["flip"] = (t[:, None] // GRID_W == t[None, :] // GRID_W) & (t[:, None] % GRID_W + t[None, :] % GRID_W == GRID_W - 1)
    out["ones"] = np.ones((P, P))
    out["slot"] = np.broadcast_to(np.arange(CAP), (P, CAP))
    out["tok"] = np.stack([NR * (t - 2 * P), NR * (t - P)], axis=1)
    place, at = {}, 0
    for k, a in out.items():
        place[k] = (at, at + a.shape[1])
        at += a.shape[1]
    masks = [((t[:, None] // m) ^ 1) == (t[None, :] // m) for m in LEVELS] + [np.eye(P) > 0]
    return (place, np.concatenate(list(out.values()), axis=1).astype(np.float32),
            np.concatenate(masks, axis=1).astype(np.float32))


def trunk_kernel(nc, A, out, place):
    stages = []
    ADA = [[("ada", 0), ("ada", 1), ("ada", 2), ("filt", 0), ("ada", 3), ("filt", 1), ("ada", 4), ("filt", 2), ("ada", 5),
            ("mod", 0), ("mod", 1), ("filtw", 0), ("filtw", 1), ("ada", 6), ("ada", 7), ("spec", 0), ("spec", 1), ("spec", 2),
            ("ada", 8), ("ada", 9), ("ada", 10), ("mod", 2), ("mod", 3), ("ada", 11)],
           [("ada", i) for i in range(6)] + [("mod", 0), ("mod", 1)] + [("ada", i) for i in range(6, 11)]
           + [("mod", 2), ("mod", 3), ("ada", 11)]]
    for l in range(2):
        stages += [((kind, i, l), 1) for kind, i in ADA[l]]
        stages += [("nab", 2)] if l == 0 else []
        stages += [(f"hTmix{l}", 4)]
        if l == 0:
            stages += [("proj0", 10), ("qkT", 9), ("att", 36)]
        else:
            stages += [("proj1", 16), ("hyena", 6)]
            for g in range(G):
                stages += [(f"glaT{g}", 3), (f"glaE{g}", 16), (f"glaS{g}", 8), (f"glaO{g}", 1)]
                if g == 0:
                    stages += [("tailE", 2), ("tailS", 2)]
        stages += [(f"oT{l}", 4), (f"out{l}", 4), (f"hTffn{l}", 4), (f"route{l}", 2), (f"tok{l}", 4), (f"pos{l}", 1)]
    J, n_jobs = {}, 0
    for name, n in stages:
        J[name] = n_jobs
        n_jobs += n

    UNITS = [(0, True, hk, 0, 4) for hk in range(2)] + [(0, False, r, 0, 4) for r in range(2)]
    UNITS += [(1, True, hk, b, 2) for hk in range(2) for b in (0, 2)]
    UNITS += [(1, False, r, b, 2) for r in range(2) for b in (0, 2)]
    NU = len(UNITS)
    ATT = []
    for u in range(NU + 2):
        ATT += [("s", u)] if u < NU else []
        ATT += [("t", u - 1)] if 0 <= u - 1 < NU else []
        ATT += [("v", u - 2)] if 0 <= u - 2 else []
    AJ = {k: J["att"] + i for i, k in enumerate(ATT)}

    ctx = ExitStack()
    with ctx:
        def sb(name, shape, dt=F32):
            return ctx.enter_context(nc.sbuf_tensor(name, shape, dt))

        def sem(name):
            return ctx.enter_context(nc.semaphore(name))

        ncst = max(b for _, b in place.values())
        cst = sb("cst", [P, ncst])
        lmask = sb("lmask", [P, 8 * P], U8)
        x = sb("x", [P, G, D])
        xn = sb("xn", [P, G, D])
        hT = sb("hT", [P, KC, G * P])
        gates = sb("gates", [P, G, 2, D])
        big = sb("big", [P, 32768])
        wring = big[:, 0:12288].rearrange("p (s n) -> p s n", s=3)
        proj = big[:, 12288:20480].rearrange("p (g n) -> p g n", g=G)
        wk = big[:, 20480:32768]
        cvec = sb("cvec", [P, G, KC])
        csg = sb("csg", [P, G, KC])
        cT = sb("cT", [P, KC, GROW + 1])
        mod = sb("mod", [P, 4, KC, G])
        gain = sb("gain", [P, 4, KC])
        wr = sb("wr", [P, KC, NE])
        rbias = sb("rbias", [P, 2, NE])
        gate = sb("gate", [P, G, NE])
        rt = sb("rt", [P, G, 2, NE])
        sel = sb("sel", [P, G, NE])
        rank = sb("rank", [P, G, NE])
        csum = sb("csum", [P, G, NE])
        pos = sb("pos", [P, G, NE])
        rk = sb("rk", [P, G, NE, 2], BF16)
        gate8 = sb("gate8", [P, NR, G])
        onehot = sb("onehot", [P, 2, G, CAP], BF16)
        idx = sb("idx", [P, U + G], I32)
        flag = sb("flag", [P, 2])
        flagi = sb("flagi", [P, 1], I32)
        st = sb("st", [P, 32])
        sink = sb("sink", [P, 8])
        att_st = sb("att_st", [P, NU, 6, 4])
        fsm = sb("fsm", [64, 4])
        nd = sb("nd", [P, P])
        rows_dram = [nc.dram_tensor(f"rows{l}", [NROW, D], F32, kind="Internal").ap() for l in range(2)]
        banks = [ctx.enter_context(nc.psum_tensor(f"bank{i}", [P, 512], F32)) for i in range(8)]

        def cs(name, a=0, n=None):
            lo, hi = place[name]
            return cst[:, lo + a:(lo + a + n if n is not None else hi)]

        ident = cs("ident")
        adarow = wk[0:GROW + 1, 0:6144]
        rot = wk[:, 0:640]
        ropet = wk[:, 640:1280].rearrange("p (a h b c) -> p a h b c", a=2, h=10, b=2)
        qkT = wk[:, 1280:1280 + 35 * P].rearrange("p (b t) -> p b t", t=P)
        pbuf = wk[:, 5760:6784].rearrange("p (a n) -> p a n", a=2)
        pTbuf = wk[:, 6784:7808].rearrange("p (a n) -> p a n", a=2)
        ck_a, cv_a = wk[:, 7808:7936], wk[:, 7936:8064]
        ck_b, cv_b = wk[:, 8064:8576], wk[:, 8576:9088]
        nab = wk[:, 9088:10112].rearrange("p (h k) -> p h k", h=8)
        nab_in = wk[:, 10240:11264].rearrange("p (h k) -> p h k", h=8)
        PQA, PQB, SQA, SQR, SQB, PKB, SKB, CKB, PKA, SKA, CKA = 0, 4, 8, 12, 16, 20, 24, 28, 32, 33, 34
        convw = wk[:, 0:6144].rearrange("p (a n) -> p a n", a=4)
        shf = wk[:, 6144:8192].rearrange("p (b a n) -> p b a n", b=2, a=2)
        hyt = wk[:, 6144:8192].rearrange("p (a n) -> p a n", a=4)
        spec = sb("spec", [P, 3, 512])
        hfil = hT[:, :, :].rearrange("p c t -> p (c t)")[:, 0:1024].rearrange("p (a n) -> p a n", a=2)
        hdif = hT[:, :, :].rearrange("p c t -> p (c t)")[:, 1024:1536]
        fact = hT[0:64, :, :].rearrange("p c t -> p (c t)")[:, 1536:2048].rearrange("p (a n) -> p a n", a=4)
        fw1 = proj[0:33, 1, 0:64]
        fw2, fw3 = proj[0:64, 1, 64:128], proj[0:64, 1, 128:192]
        dsk = proj[0:1, 1, 192:704]
        fw4 = proj[0:64, 1, 704:1728]
        lb0, lb1, lbt = wk[:, 0:1024], wk[:, 1024:2048], wk[:, 2048:3072]
        E = wk[:, 0:8192].rearrange("p (r h l t) -> p r h l t", r=2, h=NHD, l=8)
        glaT = wk[:, 8192:10240].rearrange("p (a h t) -> p a h t", a=4, h=NHD)
        accS = wk[:, 10240:10752].rearrange("p (h t) -> p h t", h=NHD)
        ob = wk[:, 10752:11264].rearrange("p (h t) -> p h t", h=NHD)
        S0 = wk[:, 11264:12288].rearrange("p (r h v) -> p r h v", r=2, h=NHD)
        QK = hT[:, :, :].rearrange("p (b a h) t -> p b a (h t)", b=2, a=2)
        gu_slot = [big[:, k * 4096:(k + 1) * 4096].rearrange("p (a c f) -> p a c f", a=2, c=KC) for k in range(U)]
        d_slot = [big[:, 16384 + k * 2048:16384 + (k + 1) * 2048].rearrange("p (c n) -> p c n", c=2) for k in range(U)]
        acc = wk[:, 10240:12288].rearrange("p (g n) -> p g n", g=G)
        xb = wk[:, 4096:7168].bitcast(BF16).rearrange("p (g a c t) -> p g a c t", g=G, a=3, c=KC)
        hg = wk[:, 7168:7168 + 2 * KC * CAP].rearrange("p (b c t) -> p b c t", b=2, c=KC)
        sgs = wk[:, 9216:9216 + 4 * CAP].rearrange("p (b n) -> p b n", b=2)
        hs = wk[:, 9728:9728 + 4 * CAP].rearrange("p (b n) -> p b n", b=2)
        split = xn
        ys = xn
        hbd = wk[:, 7168:7680]
        sgd = wk[:, 7680:8192]
        rows = ([big[:, 12288 + i * D:12288 + (i + 1) * D] for i in range(8)] + [wk[:, 6144 + i * D:6144 + (i + 1) * D] for i in range(4)]
                + [xn[:, i, :] for i in range(2)]
                + [hT[:, 4 * i:4 * i + 4, :].rearrange("p c t -> p (c t)") for i in range(2)])
        fin = wk[:, 0:2048].rearrange("p (g n) -> p g n", g=G)
        fng = wk[:, 2048:3072]

        mm_done = sem("mm_done")
        ev_done = sem("ev_done")
        cst_in = sem("cst_in")
        x_in = sem("x_in")
        small_in = sem("small_in")
        cvec_in = sem("cvec_in")
        bada_in = sem("bada_in")
        wt_in = [sem(f"wt_in{s}") for s in range(3)]
        wr_in = sem("wr_in")
        att_in = sem("att_in")
        conv_in = sem("conv_in")
        filt_in = sem("filt_in")
        gla_in = sem("gla_in")
        s0_in = sem("s0_in")
        shf_in = sem("shf_in")
        fn_in = sem("fn_in")
        gu_in = [sem(f"gu_in{k}") for k in range(U)]
        d_in = [sem(f"d_in{k}") for k in range(U)]
        kv_out, st_out, y_out = sem("kv_out"), sem("st_out"), sem("y_out")
        dve_step, act_step, pool_step = sem("dve_step"), sem("act_step"), sem("pool_step")
        c_sig, c_ready = sem("c_sig"), sem("c_ready")
        mod_ready, gate_ready = sem("mod_ready"), sem("gate_ready")
        ssq_ready, ms_ready, rt_ready = sem("ssq_ready"), sem("ms_ready"), sem("rt_ready")
        xn_ready, x_ready = sem("xn_ready"), sem("x_ready")
        rot_ready, nab_ready = sem("rot_ready"), sem("nab_ready")
        negm_ready, exp_ready, o_ready = sem("negm_ready"), sem("exp_ready"), sem("o_ready")
        split_ready, tok_ready, mask_ready = sem("split_ready"), sem("tok_ready"), sem("mask_ready")
        sh_gu, sh_sg, sh_h, sh_y, sh_out = (sem(f"sh_{k}") for k in ("gu", "sg", "h", "y", "out"))
        oh_ready = sem("oh_ready")
        hg_filled, hga_ev, hgb_ev = sem("hg_filled"), sem("hga_ev"), sem("hgb_ev")
        gu_filled, sg_ready, hid_step, h_ready = sem("gu_filled"), sem("sg_ready"), sem("hid_step"), sem("h_ready")
        y_filled, ya_ev, yb_ev, idx_ready = sem("y_filled"), sem("ya_ev"), sem("yb_ev"), sem("idx_ready")
        rows_out = [sem(f"rows_out{b}") for b in range(2)]
        scattered = sem("scattered")
        rows_in = [sem(f"rows_in{b}") for b in range(4)]
        flag_ready, over_done, over_free, sh_step = sem("flag_ready"), sem("over_done"), sem("over_free"), sem("sh_step")
        OV = [{k: sem(f"over{l}_{k}") for k in ("in", "gu", "sg", "step", "h", "y", "ya", "yb", "idx", "out")} for l in range(2)]
        farg_ready = sem("farg_ready")
        hf_ready = sem("hf_ready")
        shf_zero, shf_free, z_ready, y_spec_ready = sem("shf_zero"), sem("shf_free"), sem("z_ready"), sem("y_spec_ready")
        hy_done = sem("hy_done")
        lbd_ready, lb_ready, sg3_ready, f_ready, lf_ready, q_ready = (
            sem("lbd_ready"), sem("lb_ready"), sem("sg3_ready"), sem("f_ready"), sem("lf_ready"), sem("q_ready"))
        ksum_ready, qk_ready, qc_ready, ko_ready = sem("ksum_ready"), sem("qk_ready"), sem("qc_ready"), sem("ko_ready")
        oss_ready, oms_ready, g_ready = sem("oss_ready"), sem("oms_ready"), sem("g_ready")

        def cols(w, n):
            v = w.rearrange("(p c) n -> p c n", c=KC)
            return [v[:, :, i:min(i + 512, n)] for i in range(0, n, 512)]

        tiles = {}
        order = []
        for l in range(2):
            for name, w, n in [("ada", A["w_ada"][l], N_MOD * D),
                               ("in", A["w_in_rec"][0] if l else A["w_in_attn"][0], REC_IN if l else ATTN_IN),
                               ("out", A["w_out_rec"][0] if l else A["w_out_attn"][0], D)]:
                tiles[name, l] = len(order)
                order += cols(w, n)
        tile_job = []
        for l in range(2):
            tile_job += [J["ada", i, l] for i in range(12)]
            tile_job += [J[f"proj{l}"] + 2 * i + 1 for i in range(8 if l else 5)]
            tile_job += [J[f"out{l}"] + 2 * i + 1 for i in range(2)]

        def slot(n):
            return wring[:, n % 3, :].rearrange("p (c n) -> p c n", c=KC)[:, :, 0:order[n].shape[2]]

        def tile_ready(eng, n):
            eng.wait_ge(wt_in[n % 3], 16 * (n // 3 + 1))

        SHB = [next(b for b in range(7) if not {b, b + 1} & {(J[f"tok{l}"] + n) % 8 for n in range(5)}) for l in range(2)]

        def after(eng, s, n):
            if not isinstance(n, int) or n > 0:
                eng.wait_ge(s, n)

        def fill(pe, j):
            if j >= 8:
                pe.wait_ge(ev_done, j - 7)
            return banks[j % 8]

        def take(eng, j):
            eng.wait_ge(mm_done, j + 1)
            if j:
                eng.wait_ge(ev_done, j)
            return banks[j % 8]

        def drained(eng, j):
            eng.wait_ge(ev_done, j + 1)

        block = ctx.enter_context(nc.Block())

        @block.sync
        def _(sp):
            sp.dma_start(cvec[:, 0, :], A["c_ctx"].rearrange("(p c) -> p c", c=KC)).then_inc(cvec_in, 16)
            sp.dma_start(cvec[:, 1, :], A["c"].rearrange("a (p c) -> (a p) c", c=KC)).then_inc(cvec_in, 16)

            def load_tiles(a, b, early=()):
                for n in range(a, b):
                    if n >= 3 and n - 3 not in early:
                        sp.wait_ge(mm_done, tile_job[n - 3] + 1)
                    sp.dma_start(slot(n), order[n]).then_inc(wt_in[n % 3], 16)
                    if n == 0:
                        sp.dma_start(x[:, 0, :], A["x_prompt"][0]).then_inc(x_in, 16)
                        sp.dma_start(x[:, 1, :], A["x_sample"][0]).then_inc(x_in, 16)
                    if n == 1:
                        sp.dma_start(cst[:, :], A["cst"]).then_inc(cst_in, 16)

            def load_gate_up(k, wg, wu, s=None):
                for i, w in enumerate((wg, wu)):
                    sp.dma_start(gu_slot[k][:, i], w.rearrange("(p c) f -> p c f", c=KC)).then_inc(s or gu_in[k], 16)

            def load_down(k, wd, s=None):
                sp.dma_start(d_slot[k], wd.rearrange("(p c) n -> p c n", c=2)).then_inc(s or d_in[k], 16)

            def of(w, l, e):
                return A[w][l, bass.ds(e, 1)].rearrange("a k n -> (a k) n") if not isinstance(e, int) else A[w][l, e]

            for l in range(2):
                load_tiles(tiles["ada", l] + 3 * l, tiles["out", l] + 2)
                sp.wait_ge(mm_done, tile_job[tiles["out", l] + 1] + 1)
                sp.wait_ge(x_ready, 2 * l + 1)
                sp.wait_ge(kv_out, 64)
                load_gate_up(0, A["ws_gate"][l], A["ws_up"][l])
                load_down(0, A["ws_down"][l])

                def load(e, k):
                    at = l * NE + e
                    if isinstance(e, int) and e == 0:
                        sp.wait_ge(sh_gu, l + 1)
                    after(sp, gu_filled, at - U + 1)
                    load_gate_up(k, of("w_gate", l, e), of("w_up", l, e))
                    if isinstance(e, int) and e == 0:
                        sp.wait_ge(sh_y, l + 1)
                    after(sp, y_filled, at - U + 1)
                    load_down(k, of("w_down", l, e))

                for e in (1, 2, 3, 0):
                    load(e, e)
                with sp.Fori(1, NE // U) as i:
                    for k in range(U):
                        load(U * i + k, k)
                sp.wait_ge(flag_ready, l + 1)
                if l == 0:
                    sp.wait_ge(y_filled, (l + 1) * NE)
                sp.wait_ge(ya_ev, (l + 1) * NE)
                ov = OV[l]
                with sp.If(sp.value_load(flagi[0:1, 0:1], min_val=0, max_val=1) > 0):
                    sp.wait_ge(y_filled, (l + 1) * NE)
                    with sp.Fori(0, NE) as e:
                        sp.wait_ge(ov["y"], 4 * e)
                        load_gate_up(0, of("w_gate", l, e), of("w_up", l, e), ov["in"])
                        load_down(0, of("w_down", l, e), ov["in"])
                if l == 0:
                    load_tiles(tiles["ada", 1], tiles["ada", 1] + 1, early=range(tiles["ada", 1]))
                sp.wait_ge(over_done, l + 1)
                for n in range(G * NR):
                    g, q = n // NR, n % NR
                    src = rows_dram[l].rearrange("(t r) d -> t r d", r=NR)[g * P:(g + 1) * P, q, :]
                    sp.dma_start(rows[n], src).then_inc(rows_in[n // 4], 16)
                if l == 0:
                    load_tiles(tiles["ada", 1] + 1, tiles["ada", 1] + 3, early=range(tiles["ada", 1]))
                    sp.wait_ge(x_ready, 2)

        @block.gpsimd
        def _(pool):
            def row(src, n):
                return src.unsqueeze(0).to_broadcast([P, n])

            def after_ada(l):
                for g in range(G):
                    for i, v in enumerate((2, 5)):
                        if l and g == 0 and i == 0:
                            pool.wait_ge(x_ready, 2)
                        drained(pool, J["ada", 11, l])
                        pool.partition_broadcast(gates[:, g, i, :], adarow[GROW * g:GROW * g + 1, v * D:(v + 1) * D],
                                                 channels=P).then_inc(gate_ready, 1)

            bound = pool.to_reg(NROW - 1)

            def experts(l):
                def scatter(e, b, k):
                    at = l * NE + e
                    after(pool, ya_ev, at + 1)
                    after(pool, yb_ev, at + 1)
                    after(pool, idx_ready, at + 1)
                    pool.sem_inc(scattered, 1)
                    pool.indirect_dma_start(rows_dram[l], bass.IndirectOffsetOnAxis(ap=idx[0:CAP, k:k + 1].bitcast(U32), axis=0),
                                            ys[0:CAP, b, :], None, bounds_check=bound, oob_is_err=False).then_inc(rows_out[b], 16)

                with pool.Fori(0, NE // U) as i:
                    for k in range(U):
                        scatter(U * i + k, k % 2, k)
                for b in range(2):
                    pool.wait_ge(rows_out[b], 16 * (l + 1) * NE // 2)
                pool.wait_ge(flag_ready, l + 1)
                ov = OV[l]
                with pool.If(pool.value_load(flagi[0:1, 0:1], min_val=0, max_val=1) > 0):
                    with pool.Fori(0, NE) as e:
                        pool.wait_ge(ov["ya"], 2 * e + 2)
                        pool.wait_ge(ov["yb"], 2 * e + 2)
                        pool.wait_ge(ov["idx"], e + 1)
                        pool.sem_inc(scattered, 1)
                        for g in range(G):
                            pool.indirect_dma_start(rows_dram[l], bass.IndirectOffsetOnAxis(ap=idx[:, U + g:U + g + 1].bitcast(U32), axis=0),
                                                    ys[:, g, :], None, bounds_check=bound, oob_is_err=False).then_inc(ov["out"], 16)
                        pool.wait_ge(ov["out"], 32 * e + 32)
                pool.sem_inc(over_done, 1)

            pool.memset(cT[:, :, :], 0.0).then_inc(c_ready, 1)
            pool.dma_start(adarow, A["b_ada"][0].unsqueeze(0).to_broadcast([GROW + 1, N_MOD * D])).then_inc(bada_in, 16)
            pool.dma_start(fw1, A["filt_w1"][0]).then_inc(filt_in, 16)
            pool.dma_start(fw2, A["filt_w2"][0]).then_inc(filt_in, 16)
            pool.dma_start(fw3, A["filt_w3"][0]).then_inc(filt_in, 16)
            for i, w in enumerate(("filt_b1", "filt_b2", "filt_b3", "filt_freq")):
                pool.dma_start(fsm[:, i:i + 1], A[w][0].unsqueeze(1), allow_slow_non_contiguous=True).then_inc(filt_in, 16)
            pool.dma_start(fw4, A["filt_w4"][0]).then_inc(filt_in, 16)
            pool.dma_start(dsk, A["d_skip"]).then_inc(filt_in, 16)
            for i, (w, l) in enumerate([("norm_mix", 0), ("norm_mix", 1), ("norm_ffn", 0), ("norm_ffn", 1)]):
                pool.dma_start(gain[:, i, :], A[w][l].rearrange("(p c) -> p c", c=KC)).then_inc(small_in, 16)
            pool.dma_start(proj[:, 0, 0:8 * P], A["lmask"]).then_inc(small_in, 16)
            pool.dma_start(sink[:, :], row(A["sink_a"][0], 8)).then_inc(small_in, 16)
            for l in range(2):
                pool.dma_start(rbias[:, l, :], row(A["router_bias"][l], NE)).then_inc(small_in, 16)
            pool.dma_start(nd[:, :], row(A["norm_d"][0], P)).then_inc(small_in, 16)
            pool.dma_start(wr[:, :, :], A["w_router"][0].rearrange("(p c) e -> p c e", c=KC)).then_inc(wr_in, 16)
            for h in range(8):
                for r in range(2):
                    src = bass.AP(A["rpb_b"].tensor, (h * 15 + 7 - r) * 31 + 15 - (GRID_W - 1), [[1, GRID_W], [31, 2], [1, GRID_W]])
                    pool.dma_start(nab_in[64 * r:64 * r + 64, h, :].rearrange("p (a k) -> p a k", a=2), src).then_inc(att_in, 16)
            pool.dma_start(ck_a, A["cache_a_k"][0, 0].rearrange("t h d -> t (h d)")).then_inc(att_in, 16)
            pool.dma_start(cv_a, A["cache_a_v"][0, 0].rearrange("t h d -> t (h d)")).then_inc(att_in, 16)
            pool.dma_start(ck_b, A["cache_b_k"][0, 0].rearrange("t h d -> t (h d)")).then_inc(att_in, 16)
            pool.dma_start(cv_b, A["cache_b_v"][0, 0].rearrange("t h d -> t (h d)")).then_inc(att_in, 16)
            after_ada(0)
            drained(pool, J["proj0"] + 9)
            for o, lo, n in (("new_a_k", KA, 128), ("new_a_v", VA, 128), ("new_b_k", KB, 512), ("new_b_v", VB, 512)):
                pool.dma_start(out[o][0, 0].rearrange("t h d -> t (h d)"), proj[:, 0, lo:lo + n]).then_inc(kv_out, 16)
            experts(0)
            pool.dma_start(adarow, A["b_ada"][1].unsqueeze(0).to_broadcast([GROW + 1, N_MOD * D])).then_inc(bada_in, 16)
            pool.wait_ge(x_ready, 2)
            pool.dma_start(wr[:, :, :], A["w_router"][1].rearrange("(p c) e -> p c e", c=KC)).then_inc(wr_in, 16)
            after_ada(1)
            pool.wait_ge(gate_ready, 8)
            pool.wait_ge(mod_ready, 4)
            for i in range(3):
                pool.dma_start(convw[:, i, :], row(A["conv_w"][0, i], 1536)).then_inc(conv_in, 16)
            pool.dma_start(convw[:, 3, :], row(A["conv_b"][0], 1536)).then_inc(conv_in, 16)
            n = 0
            for g in range(G):
                for b in range(3):
                    if n == 0:
                        drained(pool, J["proj1"] + 5)
                    pool.wait_ge(shf_zero, n + 1)
                    s, c0 = n % 2, b * 512
                    for d, lo, k in ((0, 0, 112), (0, 112, 15), (1, 0, 112), (1, 112, 15)):
                        to, of = (lo + 1, lo) if d == 0 else (lo, lo + 1)
                        pool.dma_start(shf[to:to + k, s, d, :], proj[of:of + k, g, c0:c0 + 512]).then_inc(shf_in, 16)
                    pool.wait_ge(shf_in, 64 * (n + 1))
                    n += 1
            pool.wait_ge(hy_done, 1)
            pool.dma_start(lb0[:, 0:512], row(A["lb_fwd"][0], 512)).then_inc(gla_in, 16)
            pool.dma_start(lb0[:, 512:1024], row(A["lb_bwd"][0], 512)).then_inc(gla_in, 16)
            pool.dma_start(lb1[:, 0:512], row(A["lb_fwd"][1], 512)).then_inc(gla_in, 16)
            pool.dma_start(lb1[:, 512:1024], row(A["lb_bwd"][1], 512)).then_inc(gla_in, 16)
            for r, w in enumerate(("state_d_fwd", "state_d_bwd")):
                pool.dma_start(S0[:, r, :, :], A[w][0, 0].rearrange("h k v -> k h v")).then_inc(s0_in, 16)
            for r, o in enumerate(("new_d_fwd", "new_d_bwd")):
                drained(pool, J["tailS"] + r)
                pool.dma_start(out[o][0, 0].rearrange("h k v -> k h v"),
                               QK[:, 0, r, :].rearrange("p (h v) -> p h v", h=NHD)).then_inc(st_out, 16)
            experts(1)
            pool.wait_ge(x_ready, 4)
            pool.dma_start(fng, row(A["final_norm"], D)).then_inc(fn_in, 16)
            for g, o in enumerate(("y_prompt", "y_sample")):
                pool.wait_ge(xn_ready, 9 + g)
                pool.dma_start(out[o][0], fin[:, g, :]).then_inc(y_out, 16)
            pool.wait_ge(kv_out, 64)
            pool.wait_ge(st_out, 32)
            pool.wait_ge(y_out, 32)

        @block.tensor
        def _(pe):
            def transposes(stage, src, ready):
                for g in range(G):
                    ready(g)
                    for half in range(2):
                        j = J[stage] + 2 * g + half
                        bk = fill(pe, j)
                        for i in range(4):
                            v = src[:, g, :].rearrange("p (k c) -> p c k", c=KC)[:, 4 * half + i, :]
                            mm = pe.transpose(bk[:, i * P:(i + 1) * P], v, ident)
                        mm.then_inc(mm_done, 1)

            def project(stage, l, name, last_stage):
                drained(pe, last_stage)
                n0 = tiles[name, l]
                for i in range(n_of[name, l]):
                    tile_ready(pe, n0 + i)
                    w = slot(n0 + i)
                    for g in range(G):
                        bk = fill(pe, J[stage] + 2 * i + g)
                        for c in range(KC):
                            mm = pe.matmul(bk[:, 0:w.shape[2]], hT[:, c, g * P:(g + 1) * P], w[:, c, :],
                                           start=(c == 0), stop=(c == KC - 1))
                        mm.then_inc(mm_done, 1)

            n_of = {("in", 0): 5, ("in", 1): 8, ("out", 0): 2, ("out", 1): 2}

            def ada(l):
                if l == 0:
                    pe.wait_ge(c_ready, 3)
                else:
                    pe.wait_ge(over_done, 1)
                for kind, i in ADA[l]:
                    bk = fill(pe, J[kind, i, l])
                    if kind == "ada":
                        tile_ready(pe, tiles["ada", l] + i)
                        w = slot(tiles["ada", l] + i)
                        for c in range(KC):
                            mm = pe.matmul(bk[0:GROW + 1, :], cT[:, c, :], w[:, c, :], start=(c == 0), stop=(c == KC - 1))
                    elif kind == "mod":
                        pe.wait_ge(cst_in, 16)
                        v = (0, 1, 3, 4)[i]
                        drained(pe, J["ada", 2 * v + 1, l])
                        rows_v = adarow[:, v * D:(v + 1) * D].rearrange("p (k c) -> p c k", c=KC)
                        for c in range(KC):
                            mm = pe.transpose(bk[:, c * 64:c * 64 + GROW + 1], rows_v[:, c, :], ident[0:GROW + 1, 0:GROW + 1])
                    elif kind == "filt":
                        pe.wait_ge(filt_in, 16 * 9)
                        pe.wait_ge(cst_in, 16)
                        if i:
                            pe.wait_ge(hf_ready, i)
                        a = cs("zemb")[0:33, :] if i == 0 else fact[:, 3, :]
                        mm = pe.matmul(bk[0:64, 0:P], (fw1, fw2, fw3)[i], a, start=True, stop=True)
                    elif kind == "filtw":
                        pe.wait_ge(hf_ready, 3)
                        mm = pe.matmul(bk[:, :], fact[:, 3, :], fw4[:, i * 512:(i + 1) * 512], start=True, stop=True)
                    else:
                        pe.wait_ge(hf_ready, 4)
                        m, of = ((0, 0), (2, 1), (3, 0))[i]
                        mm = pe.matmul(bk[:, :], cs("dft", m * P, P), hfil[:, of, :], start=True, stop=True)
                    mm.then_inc(mm_done, 1)

            def bias_rows():
                pe.wait_ge(att_in, 16 * 20)
                for i in range(2):
                    pe.matmul(fill(pe, J["nab"] + i)[:, :], cs("flip"), nab_in[:, 4 * i:4 * i + 4, :].rearrange("p h k -> p (h k)"),
                              start=True, stop=True).then_inc(mm_done, 1)

            def attention():
                def tr(j, srcs):
                    bk = fill(pe, J["qkT"] + j)
                    for i, s in enumerate(srcs):
                        mm = pe.transpose(bk[:, i * P:(i + 1) * P], s, ident)
                    mm.then_inc(mm_done, 1)

                def b_blocks(src):
                    return [src[:, i * P:(i + 1) * P] for i in range(4)]

                drained(pe, J["proj0"] + 9)
                tr(0, b_blocks(proj[:, 0, QA:QA + 512]))
                tr(1, b_blocks(proj[:, 0, QB:QB + 512]))
                tr(2, b_blocks(proj[:, 1, QA:QA + 512]))
                pe.wait_ge(rot_ready, 1)
                tr(3, b_blocks(rot[:, 0:512]))
                tr(4, b_blocks(proj[:, 1, QB:QB + 512]))
                tr(5, b_blocks(proj[:, 0, KB:KB + 512]))
                tr(6, b_blocks(proj[:, 1, KB:KB + 512]))
                tr(7, b_blocks(ck_b))
                tr(8, [proj[:, 0, KA:KA + P], rot[:, 512:640], ck_a])
                drained(pe, J["qkT"] + 8)
                for kind, u in ATT:
                    g, is_a, half, b0, n = UNITS[u]
                    j = AJ[kind, u]
                    bk = fill(pe, j)
                    lo = 64 * half
                    for i in range(n):
                        b = b0 + i
                        if kind == "s":
                            if g == 0:
                                q, k = ((PQA + b, PKA) if is_a else (PQB + b, PKB + b))
                                parts = [(q, k, 0)]
                            elif is_a:
                                parts = [(SQA + b, CKA, 0), (SQR + b, SKA, P)]
                            else:
                                parts = [(SQB + b, CKB + b, 0), (SQB + b, SKB + b, P)]
                            w = P * len(parts)
                            for q, k, off in parts:
                                mm = pe.matmul(bk[:, i * w + off:i * w + off + P], qkT[lo:lo + 64, q, :],
                                               qkT[lo:lo + 64, k, :], start=True, stop=True)
                        elif kind == "t":
                            if i == 0:
                                drained(pe, AJ["s", u])
                                for q in range(4):
                                    mm = pe.transpose(bk[:, q * P:(q + 1) * P], pbuf[:, u % 2, q * P:(q + 1) * P], ident)
                        else:
                            if i == 0:
                                drained(pe, AJ["t", u])
                            h = 4 * half + b if is_a else 2 * b + half
                            own = (proj[:, g, VA + half * HD:VA + (half + 1) * HD] if is_a
                                   else proj[:, g, VB + h * HD:VB + (h + 1) * HD])
                            kv = half if is_a else h
                            vs = [own] if g == 0 else [(cv_a if is_a else cv_b)[:, kv * HD:(kv + 1) * HD], own]
                            for m, v in enumerate(vs):
                                c = (i * len(vs) + m) * P
                                mm = pe.matmul(bk[:, i * HD:(i + 1) * HD], pTbuf[:, u % 2, c:c + P], v,
                                               start=(m == 0), stop=(m == len(vs) - 1))
                    mm.then_inc(mm_done, 1)

            def hyena():
                for g in range(G):
                    pe.wait_ge(z_ready, g + 1)
                    for i in range(2):
                        pe.matmul(fill(pe, J["hyena"] + 3 * g + i)[:, :], cs("dft", i * P, P), proj[:, g, 512:1024],
                                  start=True, stop=True).then_inc(mm_done, 1)
                    pe.wait_ge(y_spec_ready, g + 1)
                    bk = fill(pe, J["hyena"] + 3 * g + 2)
                    for i in range(2):
                        mm = pe.matmul(bk[:, :], cs("dft", (4 + i) * P, P), hyt[:, i, :], start=(i == 0), stop=(i == 1))
                    mm.then_inc(mm_done, 1)

            def gla(g):
                pr = proj[:, g, :]
                v = pr[:, CI:CI + 512]
                pe.wait_ge(q_ready, g + 1)
                pe.wait_ge(lf_ready, g + 1)
                for i, lo in enumerate((CQ, 0, 512)):
                    bk = fill(pe, J[f"glaT{g}"] + i)
                    for h in range(NHD):
                        mm = pe.transpose(bk[:, h * P:(h + 1) * P], pr[:, lo + h * P:lo + (h + 1) * P], ident)
                    mm.then_inc(mm_done, 1)
                for r in range(2):
                    for h in range(NHD):
                        for i in range(2):
                            bk = fill(pe, J[f"glaE{g}"] + (r * NHD + h) * 2 + i)
                            lo = CF + r * 512 + h * P
                            pe.matmul(bk[:, :], pr[:, lo:lo + P], cs("expo", r * 1024 + i * 512, 512),
                                      start=True, stop=True).then_inc(mm_done, 1)
                for lev in range(8):
                    pe.wait_ge(qk_ready, 8 * g + lev + 1)
                    bk = fill(pe, J[f"glaS{g}"] + lev)
                    for h in range(NHD):
                        c = slice(h * P, (h + 1) * P)
                        if lev == 0:
                            q, k = glaT[:, 0, h, :], glaT[:, 3, h, :]
                        else:
                            q, k = QK[:, lev % 2, 0, c], QK[:, lev % 2, 1, c]
                        mm = pe.matmul(bk[:, c], k, q, start=True, stop=True)
                    mm.then_inc(mm_done, 1)
                drained(pe, J[f"glaS{g}"] + 7)
                if g == 1:
                    pe.wait_ge(qc_ready, 1)
                    pe.wait_ge(s0_in, 32)
                bk = fill(pe, J[f"glaO{g}"])
                for h in range(NHD):
                    c = slice(h * P, (h + 1) * P)
                    mm = pe.matmul(bk[:, c], accS[:, h, :], v[:, c], start=True, stop=(g == 0))
                    if g == 1:
                        pe.matmul(bk[:, c], QK[:, 0, 0, c], S0[:, 0, h, :], start=False, stop=False)
                        mm = pe.matmul(bk[:, c], QK[:, 0, 1, c], S0[:, 1, h, :], start=False, stop=True)
                mm.then_inc(mm_done, 1)
                if g == 0:
                    for r in range(2):
                        pe.matmul(fill(pe, J["tailE"] + r)[:, :], cs("tail", r * P, P), pr[:, CF + r * 512:CF + r * 512 + 512],
                                  start=True, stop=True).then_inc(mm_done, 1)
                    for r in range(2):
                        pe.wait_ge(ko_ready, r + 1)
                        bk = fill(pe, J["tailS"] + r)
                        for h in range(NHD):
                            c = slice(h * P, (h + 1) * P)
                            mm = pe.matmul(bk[:, c], pr[:, r * 512 + h * P:r * 512 + (h + 1) * P], v[:, c], start=True, stop=True)
                        mm.then_inc(mm_done, 1)

            def route(l):
                drained(pe, J[f"hTffn{l}"] + 3)
                pe.wait_ge(wr_in, 16 * (l + 1))
                for g in range(G):
                    bk = fill(pe, J[f"route{l}"] + g)
                    for c in range(KC):
                        mm = pe.matmul(bk[:, 0:NE], hT[:, c, g * P:(g + 1) * P], wr[:, c, :], start=(c == 0), stop=(c == KC - 1))
                    mm.then_inc(mm_done, 1)

            def tokens(l):
                for g in range(G):
                    for half in range(2):
                        bk = fill(pe, J[f"tok{l}"] + 2 * g + half)
                        for i in range(4):
                            mm = pe.transpose(bk[:, i * P:(i + 1) * P], hT[:, 4 * half + i, g * P:(g + 1) * P], ident)
                        mm.then_inc(mm_done, 1)

            def positions(l):
                pe.wait_ge(mask_ready, l + 1)
                bk = fill(pe, J[f"pos{l}"])
                before, ones = cs("tail", P, P), cs("ones")
                pe.matmul(bk[:, 0:NE], before, sel[:, 0, :], start=True, stop=True)
                pe.matmul(bk[:, NE:2 * NE], ones, sel[:, 0, :], start=True, stop=False)
                pe.matmul(bk[:, NE:2 * NE], before, sel[:, 1, :], start=False, stop=True)
                pe.matmul(bk[:, 2 * NE:3 * NE], ones, sel[:, 0, :], start=True, stop=False)
                pe.matmul(bk[:, 2 * NE:3 * NE], ones, sel[:, 1, :], start=False, stop=True).then_inc(mm_done, 1)

            def dense_gate_up(gu, done, b0=2):
                for i in range(2):
                    for f in range(2):
                        for c in range(KC):
                            w = gu[:, i, c, :].rearrange("p (j f) -> p f j", f=2)[:, f, :]
                            mm = pe.matmul(banks[b0 + i][:, f * 256:(f + 1) * 256], w, hT[:, c, :], start=(c == 0), stop=(c == KC - 1))
                mm.then_inc(done, 1)

            def dense_down(wd, done, each):
                for i in range(4):
                    g, half = i // 2, i % 2
                    for f in range(2):
                        mm = pe.matmul(banks[4 + i][:, :], hbd[:, f * 256 + g * P:f * 256 + (g + 1) * P],
                                       wd[:, f, half * 512:(half + 1) * 512], start=(f == 0), stop=(f == 1))
                    if each or i == 3:
                        mm.then_inc(done, 1)

            def shared_gate_up(l):
                drained(pe, J[f"route{l}"] + 1)
                pe.wait_ge(gu_in[0], 32 * l * (NE // U + 1) + 32)
                dense_gate_up(gu_slot[0], sh_gu, SHB[l])

            def shared_down(l):
                pe.wait_ge(sh_h, l + 1)
                pe.wait_ge(d_in[0], 16 * l * (NE // U + 1) + 16)
                pe.wait_ge(ev_done, J[f"pos{l}"] + 1)
                dense_down(d_slot[0], sh_y, False)

            def experts(l):
                extra = l + 1

                def gather(e, b):
                    at = l * NE + e
                    after(pe, oh_ready, at + 1)
                    after(pe, hga_ev, at)
                    after(pe, hgb_ev, at)
                    for c in range(KC):
                        o = banks[c // 4][:, (c % 4) * CAP:(c % 4 + 1) * CAP]
                        for n in range(2 * 3):
                            pe.matmul(o, xb[:, n // 3, n % 3, c, :], onehot[:, b, n // 3, :], start=(n == 0), stop=(n == 5))
                    for g in range(G):
                        mm = pe.matmul(banks[1][0:CAP, 4 * CAP:4 * CAP + 2], onehot[:, b, g, :],
                                       rk[:, g, bass.ds(e, 1), :].rearrange("p a n -> p (a n)"), start=(g == 0), stop=(g == 1))
                    mm.then_inc(hg_filled, 1)

                def gate_up(e, b, k):
                    at = l * NE + e
                    after(pe, hga_ev, at + 1)
                    after(pe, hgb_ev, at + 1)
                    after(pe, h_ready, at - 1)
                    arrived(gu_in[k], 32, e, k)
                    for i in range(2):
                        for f in range(2):
                            o = banks[2 + b][:, (2 * i + f) * CAP:(2 * i + f + 1) * CAP]
                            for c in range(KC):
                                w = gu_slot[k][:, i, c, :].rearrange("p (j f) -> p f j", f=2)[:, f, :]
                                mm = pe.matmul(o, w, hg[:, b, c, :], start=(c == 0), stop=(c == KC - 1))
                    mm.then_inc(gu_filled, 1)

                def down(e, b, k):
                    at = l * NE + e
                    after(pe, h_ready, at + 1)
                    after(pe, ya_ev, at - 1)
                    after(pe, yb_ev, at - 1)
                    arrived(d_in[k], 16, e, k)
                    for half in range(2):
                        for f in range(2):
                            mm = pe.matmul(banks[4 + 2 * b + half][0:CAP, :], hs[:, b, f * CAP:(f + 1) * CAP],
                                           d_slot[k][:, f, half * 512:(half + 1) * 512], start=(f == 0), stop=(f == 1))
                    mm.then_inc(y_filled, 1)

                def arrived(s, n, e, k):
                    i = (e - k) // U if isinstance(e, int) else None
                    fills = l * (NE // U) + (extra if k == 0 else 0) + 1
                    pe.wait_ge(s, n * (i + fills) if i is not None else (e_iter[0] * n + n * fills))

                e_iter = [None]

                def step(e, k, first=False, last=False):
                    if not last:
                        gather(e + 1, (k + 1) % 2)
                    gate_up(e, k % 2, k)
                    if not first:
                        if k == 0 and e_iter[0] is not None:
                            down_prev(e)
                        else:
                            down(e - 1, (k + 1) % 2, (k - 1) % U)

                def down_prev(e):
                    at = l * NE + e - 1
                    pe.wait_ge(h_ready, at + 1)
                    pe.wait_ge(ya_ev, at - 1)
                    pe.wait_ge(yb_ev, at - 1)
                    pe.wait_ge(d_in[U - 1], e_iter[0] * 16 + 16 * (l * (NE // U)))
                    for half in range(2):
                        for f in range(2):
                            mm = pe.matmul(banks[6 + half][0:CAP, :], hs[:, 1, f * CAP:(f + 1) * CAP],
                                           d_slot[U - 1][:, f, half * 512:(half + 1) * 512], start=(f == 0), stop=(f == 1))
                    mm.then_inc(y_filled, 1)

                pe.wait_ge(sh_out, 2 * l + 2)
                pe.wait_ge(tok_ready, 4 * l + 4)
                gather(0, 0)
                for k in range(U):
                    step(k, k, first=(k == 0))
                with pe.Fori(1, NE // U - 1) as i:
                    e_iter[0] = i
                    for k in range(U):
                        step(U * i + k, k)
                e_iter[0] = None
                for k in range(U):
                    step(NE - U + k, k, last=(k == U - 1))
                down(NE - 1, 1, U - 1)
                pe.wait_ge(flag_ready, l + 1)
                pe.wait_ge(ya_ev, (l + 1) * NE)
                pe.wait_ge(yb_ev, (l + 1) * NE)
                ov = OV[l]
                with pe.If(pe.value_load(flagi[0:1, 0:1], min_val=0, max_val=1) > 0):
                    with pe.Fori(0, NE) as e:
                        pe.wait_ge(ov["in"], 48 * e + 48)
                        pe.wait_ge(ov["h"], e)
                        dense_gate_up(gu_slot[0], ov["gu"])
                        pe.wait_ge(ov["h"], e + 1)
                        pe.wait_ge(ov["ya"], 2 * e)
                        pe.wait_ge(ov["yb"], 2 * e)
                        dense_down(d_slot[0], ov["y"], True)

            for l in range(2):
                ada(l)
                if l == 0:
                    bias_rows()
                transposes(f"hTmix{l}", xn, lambda g: pe.wait_ge(xn_ready, 4 * l + g + 1))
                project(f"proj{l}", l, "in", J[f"hTmix{l}"] + 3)
                if l == 0:
                    attention()
                    ready = lambda g: drained(pe, AJ["v", NU - 1])
                else:
                    hyena()
                    gla(0)
                    gla(1)
                    ready = lambda g: pe.wait_ge(o_ready, g + 1)
                transposes(f"oT{l}", xn, ready)
                project(f"out{l}", l, "out", J[f"oT{l}"] + 3)
                transposes(f"hTffn{l}", xn, lambda g: pe.wait_ge(xn_ready, 4 * l + 2 + g + 1))
                route(l)
                tokens(l)
                shared_gate_up(l)
                positions(l)
                shared_down(l)
                experts(l)

        @block.scalar
        def _(act):
            steps = [0]

            def link(ins):
                steps[0] += 1
                ins.then_inc(act_step, 1)
                act.wait_ge(act_step, steps[0])

            def sumsq(n):
                g = n % 2
                act.wait_ge(x_ready, n // 2) if n >= 2 else act.wait_ge(x_in, 32)
                if n >= 8:
                    dst = fin[:, g, :]
                else:
                    dst = xn[:, g, :]
                if 2 <= n < 8:
                    stage = ["", "out0", "hTffn0", "out1"][n // 2]
                    act.wait_ge(mm_done, J[stage] + 4)
                act.activation(dst, x[:, g, :], ACT.Square, accum_out=st[:, 2 * g:2 * g + 1]).then_inc(ssq_ready, 1)
                act.wait_ge(ms_ready, n + 1)
                act.activation(st[:, 2 * g + 1:2 * g + 2], st[:, 2 * g:2 * g + 1], ACT.Sqrt).then_inc(rt_ready, 1)

            def to_hT(stage, l, which):
                act.wait_ge(mod_ready, 2 * l + which + 1)
                for g in range(G):
                    for half in range(2):
                        j = J[stage] + 2 * g + half
                        bk = take(act, j)
                        for i in range(4):
                            c = 4 * half + i
                            a = act.activation(hT[:, c, g * P:(g + 1) * P], bk[:, i * P:(i + 1) * P], ACT.Identity,
                                               bias=mod[:, 2 * which, c, g:g + 1], scale=mod[:, 2 * which + 1, c, g:g + 1])
                            link(a) if i < 3 else a.then_inc(ev_done, 1)

            def copy_job(j, dst, n=512):
                bk = take(act, j)
                act.activation(dst, bk[:, 0:n], ACT.Copy).then_inc(ev_done, 1)

            def oT(l):
                for g in range(G):
                    for half in range(2):
                        j = J[f"oT{l}"] + 2 * g + half
                        bk = take(act, j)
                        act.activation(hT[:, 4 * half:4 * half + 4, g * P:(g + 1) * P],
                                       bk[:, :].rearrange("p (c t) -> p c t", c=4), ACT.Copy).then_inc(ev_done, 1)

            def softmaxes():
                for u in range(NU):
                    g, is_a, half, b0, n = UNITS[u]
                    w = 512 // n
                    act.wait_ge(negm_ready, u + 1)
                    bk = take(act, AJ["s", u])
                    if u >= 2:
                        act.wait_ge(mm_done, AJ["t", u - 2] + 1)
                    s = att_st[:, u]
                    for i in range(n):
                        a = act.activation(pbuf[:, u % 2, i * w:(i + 1) * w], bk[:, i * w:(i + 1) * w], ACT.Exp,
                                           bias=s[:, 1, i:i + 1], accum_out=s[:, 2, i:i + 1])
                        link(a) if (i < n - 1 or is_a) else a.then_inc(ev_done, 1)
                    if is_a:
                        act.activation(s[:, 4, 0:n], s[:, 3, 0:n], ACT.Exp).then_inc(ev_done, 1)

            def gla_gates():
                act.wait_ge(lbd_ready, 1)
                act.activation(lb0, lbt, ACT.Sigmoid).then_inc(lb_ready, 1)
                act.activation(lb1, lbt, ACT.Sigmoid, scale=-1.0).then_inc(lb_ready, 1)
                act.wait_ge(lb_ready, 2)
                for g in range(G):
                    pr = proj[:, g, :]
                    act.activation(pr[:, 0:1024], pr[:, CF:CF + 1024], ACT.Sigmoid, scale=-1.0).then_inc(sg3_ready, 1)
                    act.wait_ge(sg3_ready, 4 * g + 1)
                    act.activation(pr[:, CF:CF + 1024], pr[:, CF:CF + 1024], ACT.Sigmoid).then_inc(sg3_ready, 1)
                    act.activation(lbt[:, 0:512] if g == 0 else ob4, pr[:, CQ:CQ + 512], ACT.Sigmoid).then_inc(sg3_ready, 1)
                    act.activation(pr[:, 1024:1536], pr[:, CG:CG + 512], ACT.Sigmoid).then_inc(sg3_ready, 1)
                for g in range(G):
                    pr = proj[:, g, :]
                    act.wait_ge(f_ready, g + 1)
                    act.activation(pr[:, CF:CF + 1024], pr[:, CF:CF + 1024], ACT.Ln).then_inc(lf_ready, 1)

            ob4 = wk[:, 3072:3584]

            def gla(g):
                for i in range(3):
                    copy_job(J[f"glaT{g}"] + i, glaT[:, i, :, :].rearrange("p h t -> p (h t)"))
                act.wait_ge(q_ready, 2)
                for r in range(2):
                    for h in range(NHD):
                        for i in range(2):
                            bk = take(act, J[f"glaE{g}"] + (r * NHD + h) * 2 + i)
                            act.activation(E[:, r, h, 4 * i:4 * i + 4, :].rearrange("p l t -> p (l t)"), bk[:, :],
                                           ACT.Exp).then_inc(ev_done, 1)
                if g == 0:
                    for r in range(2):
                        bk = take(act, J["tailE"] + r)
                        act.activation(QK[:, 1, r, :], bk[:, :], ACT.Exp).then_inc(ev_done, 1)
                    for r in range(2):
                        copy_job(J["tailS"] + r, QK[:, 0, r, :])
                act.wait_ge(oss_ready, g + 1)
                act.activation(st[:, 8 + 4 * g:12 + 4 * g], st[:, 16 + 4 * g:20 + 4 * g], ACT.Sqrt).then_inc(oms_ready, 1)

            def route(l):
                for g in range(G):
                    bk = take(act, J[f"route{l}"] + g)
                    if l:
                        act.wait_ge(tok_ready, 4)
                    act.activation(rt[:, g, 0, :], bk[:, 0:NE], ACT.Sigmoid).then_inc(ev_done, 1)

            def tokens(l):
                for n in range(4):
                    act.wait_ge(mm_done, J[f"tok{l}"] + n + 1)
                    bk = banks[(J[f"tok{l}"] + n) % 8]
                    act.activation(xb[:, n // 2, 0, 4 * (n % 2):4 * (n % 2) + 4, :].rearrange("p c t -> p (c t)"), bk[:, :],
                                   ACT.Copy).then_inc(split_ready, 1)

            def dense_sigmoid(s, b0=2):
                act.activation(sgd, banks[b0][:, :], ACT.Sigmoid).then_inc(s, 1)

            def experts(l):
                act.wait_ge(sh_gu, l + 1)
                dense_sigmoid(sh_sg, SHB[l])
                act.wait_ge(sh_y, l + 1)
                for half in range(2):
                    ins = act.activation(acc[:, 0, half * 512:(half + 1) * 512], banks[4 + half][:, :], ACT.Copy)
                    if half:
                        ins.then_inc(sh_out, 1)

                def half_a(e, b):
                    at = l * NE + e
                    after(act, hg_filled, at + 1)
                    after(act, gu_filled, at - 1)
                    act.activation(hg[:, b, 0:4, :], banks[0][:, 0:4 * CAP].rearrange("p (c t) -> p c t", c=4),
                                   ACT.Copy).then_inc(hga_ev, 1)

                def sig(e, b):
                    after(act, gu_filled, l * NE + e + 1)
                    act.activation(sgs[:, b, :], banks[2 + b][:, 0:2 * CAP], ACT.Sigmoid).then_inc(sg_ready, 1)

                def rows_a(e, b, sent):
                    after(act, y_filled, l * NE + e + 1)
                    after(act, rows_out[b], sent)
                    act.activation(ys[0:CAP, b, 0:512], banks[4 + 2 * b][0:CAP, :], ACT.Copy).then_inc(ya_ev, 1)

                def steps_of(e0, first=False, last=False, i=None):
                    for k in range(U):
                        e = e0 + k
                        if not (last and k == U - 1):
                            half_a(e + 1, (k + 1) % 2)
                        sig(e, k % 2)
                        if not (first and k == 0):
                            rows_a(e - 1, (k + 1) % 2, sent_before(e, i, k))

                def sent_before(e, i, k):
                    done = 16 * l * NE // 2
                    if i is None:
                        return done + 16 * ((e - 1) // 2)
                    return i * (16 * U // 2) + (done + 16 * ((k - 1) // 2))

                half_a(0, 0)
                steps_of(0, first=True)
                with act.Fori(1, NE // U - 1) as i:
                    steps_of(U * i, i=i)
                steps_of(NE - U, last=True)
                rows_a(NE - 1, 1, 16 * l * NE // 2 + 16 * ((NE - 1) // 2))
                act.wait_ge(flag_ready, l + 1)
                act.wait_ge(over_free, l + 1)
                ov = OV[l]
                with act.If(act.value_load(flagi[0:1, 0:1], min_val=0, max_val=1) > 0):
                    with act.Fori(0, NE) as e:
                        act.wait_ge(ov["gu"], e + 1)
                        dense_sigmoid(ov["sg"])
                        for i in range(2):
                            act.wait_ge(ov["y"], 4 * e + i + 1)
                            if i == 0:
                                act.wait_ge(ov["out"], 32 * e)
                            act.activation(ys[:, 0, i * 512:(i + 1) * 512], banks[4 + i][:, :], ACT.Copy).then_inc(ov["ya"], 1)

            act.wait_ge(cvec_in, 32)
            act.activation(csg[:, :, :], cvec[:, :, :], ACT.Sigmoid).then_inc(c_sig, 1)
            for l in range(2):
                sumsq(4 * l)
                sumsq(4 * l + 1)
                if l == 0:
                    for i in range(3):
                        act.wait_ge(farg_ready, i + 1)
                        act.activation(fact[:, 3, :], fact[:, 0, :], ACT.Sin).then_inc(hf_ready, 1)
                    for i in range(3):
                        copy_job(J["spec", i, 0], spec[:, i, :])
                to_hT(f"hTmix{l}", l, 0)
                if l == 0:
                    for i in range(10):
                        n = 512 if i < 8 else 256
                        if i < G:
                            bk = take(act, J["proj0"] + i)
                            act.activation(proj[:, i, 0:512].rearrange("p (h k d) -> p k h d", k=2, d=HD),
                                           bk[:, :].rearrange("p (k h d) -> p k h d", k=2, d=HD), ACT.Copy).then_inc(ev_done, 1)
                            continue
                        copy_job(J["proj0"] + i, proj[:, i % 2, (i // 2) * 512:(i // 2) * 512 + n], n)
                    softmaxes()
                else:
                    act.wait_ge(kv_out, 64)
                    for i in range(16):
                        copy_job(J["proj1"] + i, proj[:, i % 2, (i // 2) * 512:(i // 2) * 512 + 512])
                    gla_gates()
                    gla(0)
                    act.wait_ge(st_out, 32)
                    gla(1)
                oT(l)
                sumsq(4 * l + 2)
                sumsq(4 * l + 3)
                to_hT(f"hTffn{l}", l, 1)
                route(l)
                tokens(l)
                experts(l)
            sumsq(8)
            sumsq(9)

        @block.vector
        def _(dve):
            steps = [0]

            def link(ins):
                steps[0] += 1
                ins.then_inc(dve_step, 1)
                dve.wait_ge(dve_step, steps[0])

            def norm(n):
                g = n % 2
                s = st[:, 2 * g:2 * g + 1]
                dve.wait_ge(ssq_ready, n + 1)
                dve.tensor_scalar(s, s, 1.0 / D, EPS, ALU.mult, ALU.add).then_inc(ms_ready, 1)
                dve.wait_ge(rt_ready, n + 1)
                link(dve.reciprocal(st[:, 4 + g:5 + g], st[:, 2 * g + 1:2 * g + 2]))
                if n < 8:
                    dve.tensor_scalar(xn[:, g, :], x[:, g, :], st[:, 4 + g:5 + g], None, ALU.mult).then_inc(xn_ready, 1)
                else:
                    dve.wait_ge(fn_in, 16)
                    dve.scalar_tensor_tensor(out=fin[:, g, :], in0=x[:, g, :], scalar=st[:, 4 + g:5 + g], in1=fng,
                                             op0=ALU.mult, op1=ALU.mult).then_inc(xn_ready, 1)

            def ada(l):
                dve.wait_ge(bada_in, 16 * (l + 1))
                dve.wait_ge(small_in, 16 * 9)
                for kind, i in ADA[l]:
                    j = J[kind, i, l]
                    if kind == "ada":
                        bk = take(dve, j)
                        c = slice(i * 512, (i + 1) * 512)
                        dve.tensor_tensor(adarow[:, c], bk[0:GROW + 1, :], adarow[:, c], ALU.add).then_inc(ev_done, 1)
                    elif kind == "mod":
                        bk = take(dve, j)
                        src = bk[:, :].rearrange("p (c r) -> p c r", c=KC)[:, :, 0:GROW + 1:GROW]
                        dve.tensor_copy(mod[:, i, :, :], src).then_inc(ev_done, 1)
                        if i % 2:
                            drained(dve, j)
                            link(dve.tensor_scalar(mod[:, i, :, :], mod[:, i, :, :], 1.0, None, ALU.add))
                            for g in range(G):
                                m = mod[:, i, :, g]
                                link(dve.tensor_tensor(m, m, gain[:, 2 * (i // 2) + l, :], ALU.mult))
                            dve.sem_inc(mod_ready, 1)
                    elif kind == "filt":
                        filter_layer(i)
                    elif kind == "filtw":
                        filter_taps(i)

            def filter_layer(i):
                j = J["filt", i, 0]
                bk = take(dve, j)
                a, k = fact[:, 0, :], fact[:, 1, :]
                dve.tensor_scalar(a, bk[0:64, 0:P], fsm[:, i:i + 1], fsm[:, 3:4], ALU.add, ALU.mult).then_inc(ev_done, 1)
                drained(dve, j)
                link(dve.tensor_scalar(k, a, 1.0 / TWO_PI, MAGIC, ALU.mult, ALU.add))
                link(dve.tensor_scalar(k, k, MAGIC, None, ALU.subtract))
                for part in (PI_1, PI_2, PI_3):
                    link(dve.scalar_tensor_tensor(out=a, in0=k, scalar=-part, in1=a, op0=ALU.mult, op1=ALU.add))
                dve.tensor_scalar(a, a, 3.1415925, -3.1415925, ALU.min, ALU.max).then_inc(farg_ready, 1)

            def filter_taps(i):
                j = J["filtw", i, 0]
                if i == 0:
                    dve.wait_ge(filt_in, 16 * 9)
                bk = take(dve, j)
                dve.tensor_tensor(hfil[:, i, :], bk[:, :], cs("window"), ALU.mult).then_inc(ev_done, 1)
                if i == 0:
                    return
                drained(dve, j)
                link(dve.tensor_tensor(hdif, hfil[:, 0, :], hfil[:, 1, :], ALU.subtract))
                link(dve.tensor_tensor(hfil[:, 0, :], hfil[:, 0, :], hfil[:, 1, :], ALU.add))
                link(dve.tensor_tensor(hfil[0:1, 0, :], hfil[0:1, 0, :], dsk, ALU.add))
                dve.tensor_copy(hfil[:, 1, :], hdif).then_inc(hf_ready, 1)

            def bias_rows():
                for i in range(2):
                    bk = take(dve, J["nab"] + i)
                    dve.tensor_tensor(nab[:, 4 * i:4 * i + 4, :], bk[:, :].rearrange("p (h k) -> p h k", h=4),
                                      cs("namask").unsqueeze(1).to_broadcast([P, 4, P]), ALU.add).then_inc(ev_done, 1)

            def rope():
                drained(dve, J["proj0"] + 3)
                dve.wait_ge(gate_ready, 4)
                v = proj[:, 1, 0:640].rearrange("p (h b x c) -> p h b x c", h=10, b=2, x=2)
                o = rot.rearrange("p (h b x c) -> p h b x c", h=10, b=2, x=2)
                cos, sin = [cs("rope", a * 32, 32).rearrange("p (b c) -> p b c", b=2) for a in range(2)]

                def bc(t, b):
                    return t[:, b, :].unsqueeze(1).to_broadcast([P, 10, 16])

                t1, t2 = ropet[:, 0], ropet[:, 1]
                for xo, first, second, op in ((0, cos, sin, ALU.subtract), (1, sin, cos, ALU.add)):
                    for b in range(2):
                        link(dve.tensor_tensor(t1[:, :, b, :], v[:, :, b, 0, :], bc(first, b), ALU.mult))
                        link(dve.tensor_tensor(t2[:, :, b, :], v[:, :, b, 1, :], bc(second, b), ALU.mult))
                        link(dve.tensor_tensor(o[:, :, b, xo, :], t1[:, :, b, :], t2[:, :, b, :], op))
                dve.sem_inc(rot_ready, 1)

            def attention():
                for j in range(9):
                    n = 4 if j < 8 else 3
                    bk = take(dve, J["qkT"] + j)
                    dve.tensor_scalar(qkT[:, 4 * j:4 * j + n, :], bk[:, 0:n * P].rearrange("p (b t) -> p b t", t=P),
                                      HD ** -0.5 if j < 5 else 1.0, None, ALU.mult).then_inc(ev_done, 1)

                def scores(u):
                    g, is_a, half, b0, n = UNITS[u]
                    bk = banks[AJ["s", u] % 8]
                    dve.wait_ge(mm_done, AJ["s", u] + 1)
                    S = bk[:, :].rearrange("p (h k) -> p h k", h=n)
                    if g == 1 and not is_a:
                        hs = nab.rearrange("p (b r) k -> p b r k", r=2)[:, b0:b0 + n, half, :]
                        link(dve.tensor_tensor(S[:, :, P:2 * P], S[:, :, P:2 * P], hs, ALU.add))
                    s = att_st[:, u]
                    link(dve.tensor_reduce(s[:, 0, 0:n], S, AX, ALU.max))
                    if is_a:
                        sk = sink[:, 4 * half + b0:4 * half + b0 + n]
                        link(dve.tensor_tensor(s[:, 0, 0:n], s[:, 0, 0:n], sk, ALU.max))
                        link(dve.tensor_tensor(s[:, 3, 0:n], sk, s[:, 0, 0:n], ALU.subtract))
                    dve.tensor_scalar(s[:, 1, 0:n], s[:, 0, 0:n], -1.0, None, ALU.mult).then_inc(negm_ready, 1)

                def denominators(u):
                    g, is_a, half, b0, n = UNITS[u]
                    s = att_st[:, u]
                    drained(dve, AJ["s", u])
                    if is_a:
                        link(dve.tensor_tensor(s[:, 2, 0:n], s[:, 2, 0:n], s[:, 4, 0:n], ALU.add))
                    link(dve.reciprocal(s[:, 5, 0:n], s[:, 2, 0:n]))

                def values(u):
                    g, is_a, half, b0, n = UNITS[u]
                    bk = take(dve, AJ["v", u])
                    dst = xn[:, g, 0:512].rearrange("p (k b d) -> p k b d", k=2, d=HD)[:, half, b0:b0 + n, :] if is_a else \
                        xn[:, g, 512:1024].rearrange("p (b r d) -> p r b d", r=2, d=HD)[:, half, b0:b0 + n, :]
                    dve.tensor_tensor(dst, bk[:, 0:n * HD].rearrange("p (b d) -> p b d", d=HD),
                                      att_st[:, u, 5, 0:n].unsqueeze(2).to_broadcast([P, n, HD]), ALU.mult).then_inc(ev_done, 1)

                for kind, u in ATT:
                    if kind == "s":
                        scores(u)
                    elif kind == "t":
                        bk = take(dve, AJ["t", u])
                        if u >= 2:
                            dve.wait_ge(mm_done, AJ["v", u - 2] + 1)
                        dve.tensor_copy(pTbuf[:, u % 2, :], bk[:, :]).then_inc(ev_done, 1)
                    else:
                        denominators(u)
                        values(u)

            def add_out(l):
                dve.wait_ge(gate_ready, 4 * l + 4)
                for i in range(4):
                    bk = take(dve, J[f"out{l}"] + i)
                    g, c = i % 2, slice((i // 2) * 512, (i // 2) * 512 + 512)
                    tmp = wk[:, i * 512:(i + 1) * 512]
                    dve.tensor_tensor(tmp, bk[:, :], gates[:, g, 0, c], ALU.mult).then_inc(ev_done, 1)
                    drained(dve, J[f"out{l}"] + i)
                    link(dve.tensor_tensor(x[:, g, c], x[:, g, c], tmp, ALU.add))
                dve.sem_inc(x_ready, 1)

            def top8(l):
                for g in range(G):
                    drained(dve, J[f"route{l}"] + g)
                    sc, bi = rt[:, g, 0, :], rt[:, g, 1, :]
                    sl = sel[:, g, :]
                    link(dve.tensor_tensor(bi, sc, rbias[:, l, :], ALU.add))
                    link(dve.max(out=st[:, 24:32], in_=bi))
                    link(dve.match_replace(out=sl, in_to_replace=st[:, 24:32], in_values=bi, imm_value=-BIG))
                    ins = dve.tensor_tensor(sl, sl, bi, ALU.not_equal)
                    if g == 1:
                        ins.then_inc(mask_ready, 1)
                        dve.wait_ge(mask_ready, l + 1)
                    else:
                        link(ins)
                    link(dve.tensor_tensor(gate[:, g, :], sl, sc, ALU.mult))
                    link(dve.tensor_reduce(st[:, 6:7], gate[:, g, :], AX, ALU.add))
                    link(dve.reciprocal(st[:, 7:8], st[:, 6:7]))
                    link(dve.tensor_scalar(gate[:, g, :], gate[:, g, :], st[:, 7:8], 2.5, ALU.mult, ALU.mult))

            def ranks():
                src = sel[:, :, :]
                for n, d in enumerate((1, 2, 4, 8, 16, 32)):
                    dst = (rank, csum)[n % 2][:, :, :]
                    link(dve.tensor_copy(dst[:, :, 0:d], src[:, :, 0:d]))
                    link(dve.tensor_tensor(dst[:, :, d:NE], src[:, :, d:NE], src[:, :, 0:NE - d], ALU.add))
                    src = dst
                link(dve.tensor_tensor(rank[:, :, :], csum[:, :, :], sel[:, :, :], ALU.subtract))
                link(dve.tensor_copy(rk[:, :, :, 0], cs("tok").unsqueeze(2).to_broadcast([P, G, NE])))
                link(dve.tensor_copy(rk[:, :, :, 1], rank[:, :, :]))
                for q in range(NR):
                    link(dve.tensor_scalar(csum[:, :, :], rank[:, :, :], float(q), None, ALU.is_equal))
                    link(dve.tensor_tensor(csum[:, :, :], csum[:, :, :], gate[:, :, :], ALU.mult))
                    link(dve.tensor_reduce(gate8[:, q, :], csum[:, :, :], AX, ALU.add))

            def positions(l):
                bk = take(dve, J[f"pos{l}"])
                link(dve.scalar_tensor_tensor(out=pos[:, :, :], in0=bk[:, 0:2 * NE].rearrange("p (g e) -> p g e", g=G), scalar=1.0,
                                              in1=sel[:, :, :], op0=ALU.add, op1=ALU.mult))
                link(dve.tensor_scalar(pos[:, :, :], pos[:, :, :], 1.0, None, ALU.subtract))
                dve.tensor_reduce(flag[:, 0:1], bk[:, 2 * NE:3 * NE], AX, ALU.max).then_inc(ev_done, 1)
                dve.wait_ge(ev_done, J[f"pos{l}"] + 1)
                dve.tensor_scalar(flagi[:, :], flag[:, 0:1], float(CAP), None, ALU.is_gt).then_inc(flag_ready, 1)

            def tokens(l):
                for n in range(4):
                    g, cc = n // 2, slice(4 * (n % 2), 4 * (n % 2) + 4)
                    part = [xb[:, g, a, cc, :].rearrange("p c t -> p (c t)") for a in range(3)]
                    rem = split[:, g, (n % 2) * 512:(n % 2) * 512 + 512]
                    dve.wait_ge(split_ready, 4 * l + n + 1)
                    bk = take(dve, J[f"tok{l}"] + n)
                    dve.tensor_tensor(rem, bk[:, :], part[0], ALU.subtract).then_inc(ev_done, 1)
                    drained(dve, J[f"tok{l}"] + n)
                    link(dve.tensor_copy(part[1], rem))
                    link(dve.tensor_tensor(rem, rem, part[1], ALU.subtract))
                    dve.tensor_copy(part[2], rem).then_inc(tok_ready, 1)
                dve.wait_ge(tok_ready, 4 * l + 4)

            def dense_hidden(sg, n_sg, step, n_step, done, b0=2):
                dve.wait_ge(sg, n_sg)
                dve.tensor_tensor(sgd, sgd, banks[b0][:, :], ALU.mult).then_inc(step, 1)
                dve.wait_ge(step, n_step)
                dve.tensor_tensor(hbd, sgd, banks[b0 + 1][:, :], ALU.mult).then_inc(done, 1)

            def shared_out(l):
                dve.wait_ge(sh_y, l + 1)
                for half in range(2):
                    ins = dve.tensor_copy(acc[:, 1, half * 512:(half + 1) * 512], banks[6 + half][:, :])
                    if half:
                        ins.then_inc(sh_out, 1)

            def experts(l):
                def columns(e, b):
                    at = l * NE + e
                    after(dve, hg_filled, at - 1)
                    for g in range(G):
                        ins = dve.tensor_scalar(onehot[:, b, g, :], cs("slot"), pos[:, g, bass.ds(e, 1)], None, ALU.is_equal)
                    ins.then_inc(oh_ready, 1)

                def half_b(e, b, k, sent):
                    at = l * NE + e
                    after(dve, hg_filled, at + 1)
                    after(dve, gu_filled, at - 1)
                    after(dve, rows_out[b], sent)
                    dve.tensor_scalar(idx[0:CAP, k:k + 1], banks[1][0:CAP, 4 * CAP:4 * CAP + 1], idx_hi[:, 0:1], float(SKIP),
                                      ALU.add, ALU.add).then_inc(idx_ready, 1)
                    dve.tensor_copy(hg[:, b, 4:8, :], banks[1][:, 0:4 * CAP].rearrange("p (c t) -> p c t", c=4)).then_inc(hgb_ev, 1)

                idx_hi = banks[1][0:CAP, 4 * CAP + 1:4 * CAP + 2]

                def hidden(e, b):
                    at = l * NE + e
                    after(dve, sg_ready, at + 1)
                    dve.tensor_tensor(sgs[:, b, :], sgs[:, b, :], banks[2 + b][:, 0:2 * CAP], ALU.mult).then_inc(hid_step, 1)
                    after(dve, hid_step, at + 1)
                    dve.tensor_tensor(hs[:, b, :], sgs[:, b, :], banks[2 + b][:, 2 * CAP:4 * CAP], ALU.mult).then_inc(h_ready, 1)

                def rows_b(e, b, sent):
                    after(dve, y_filled, l * NE + e + 1)
                    after(dve, rows_out[b], sent)
                    dve.tensor_copy(ys[0:CAP, b, 512:1024], banks[5 + 2 * b][0:CAP, :]).then_inc(yb_ev, 1)

                def sent(i, e):
                    done = 16 * l * NE // 2 + 16 * (e // 2)
                    return done if i is None else i * (16 * U // 2) + done

                def steps_of(e0, first=False, last=False, i=None):
                    for k in range(U):
                        e = e0 + k
                        ek = e if i is None else k
                        if not (last and k >= U - 2):
                            columns(e + 2, k % 2)
                        if not (last and k == U - 1):
                            half_b(e + 1, (k + 1) % 2, (k + 1) % U, sent(i, ek - 1))
                        hidden(e, k % 2)
                        if not (first and k == 0):
                            rows_b(e - 1, (k + 1) % 2, sent(i, ek - 1))

                columns(0, 0)
                columns(1, 1)
                half_b(0, 0, 0, 16 * l * NE // 2)
                steps_of(0, first=True)
                with dve.Fori(1, NE // U - 1) as i:
                    steps_of(U * i, i=i)
                steps_of(NE - U, last=True)
                rows_b(NE - 1, 1, sent(None, NE - 1))
                overflow(l)
                for g in range(G):
                    for q in range(NR):
                        dve.wait_ge(rows_in[(g * NR + q) // 4], 64 * (l + 1))
                        link(dve.scalar_tensor_tensor(out=acc[:, g, :], in0=rows[g * NR + q], scalar=gate8[:, q, g:g + 1],
                                                      in1=acc[:, g, :], op0=ALU.mult, op1=ALU.add))
                    link(dve.tensor_tensor(acc[:, g, :], acc[:, g, :], gates[:, g, 1, :], ALU.mult))
                    link(dve.tensor_tensor(x[:, g, :], x[:, g, :], acc[:, g, :], ALU.add))
                dve.sem_inc(x_ready, 1)

            def overflow(l):
                ov = OV[l]
                dve.wait_ge(yb_ev, (l + 1) * NE)
                dve.wait_ge(flag_ready, l + 1)
                for b in range(2):
                    dve.wait_ge(rows_out[b], 16 * (l + 1) * NE // 2)
                dve.sem_inc(over_free, 1)
                with dve.If(dve.value_load(flagi[0:1, 0:1], min_val=0, max_val=1) > 0):
                    over = csum[:, :, :]
                    dve.tensor_scalar(over, pos[:, :, :], float(CAP) - 0.5, None, ALU.is_gt).then_inc(ov["step"], 1)
                    dve.wait_ge(ov["step"], 1)
                    dve.tensor_tensor(pos[:, :, :], rank[:, :, :], cs("tok").unsqueeze(2).to_broadcast([P, G, NE]),
                                      ALU.add).then_inc(ov["step"], 1)
                    dve.wait_ge(ov["step"], 2)
                    dve.tensor_tensor(pos[:, :, :], pos[:, :, :], over, ALU.mult).then_inc(ov["step"], 1)
                    dve.wait_ge(ov["step"], 3)
                    with dve.Fori(0, NE) as e:
                        dense_hidden(ov["sg"], e + 1, ov["step"], e + 4, ov["h"])
                        dve.wait_ge(ov["out"], 32 * e)
                        for g in range(G):
                            ins = dve.tensor_scalar(idx[:, U + g:U + g + 1], pos[:, g, bass.ds(e, 1)], float(SKIP), None, ALU.add)
                        ins.then_inc(ov["idx"], 1)
                        for i in range(2):
                            dve.wait_ge(ov["y"], 4 * e + 3 + i)
                            dve.tensor_copy(ys[:, 1, i * 512:(i + 1) * 512], banks[6 + i][:, :]).then_inc(ov["yb"], 1)

            def hyena():
                n = 0
                for g in range(G):
                    for b in range(3):
                        s = n % 2
                        link(dve.memset(shf[:, s, :, :], 0.0))
                        dve.sem_inc(shf_zero, 1)
                        dve.wait_ge(shf_in, 64 * (n + 1))
                        dve.wait_ge(conv_in, 64)
                        c = slice(b * 512, (b + 1) * 512)
                        u = proj[:, g, c]
                        link(dve.tensor_tensor(u, u, convw[:, 1, c], ALU.mult))
                        for d, tap in ((0, 0), (1, 2)):
                            link(dve.tensor_tensor(shf[:, s, d, :], shf[:, s, d, :], convw[:, tap, c], ALU.mult))
                            link(dve.tensor_tensor(u, u, shf[:, s, d, :], ALU.add))
                        link(dve.tensor_tensor(u, u, convw[:, 3, c], ALU.add))
                        n += 1
                    z = proj[:, g, 512:1024]
                    dve.tensor_tensor(z, z, proj[:, g, 1024:1536], ALU.mult).then_inc(z_ready, 1)
                    j = J["hyena"] + 3 * g
                    sA, sB, sD = (spec[:, i, :] for i in range(3))
                    yr, yi, t = hyt[:, 0, :], hyt[:, 1, :], hyt[:, 2, :]
                    zr = take(dve, j)
                    link(dve.tensor_tensor(yr, zr[:, :], sA, ALU.mult))
                    dve.tensor_tensor(yi, zr[:, :], sB, ALU.mult).then_inc(ev_done, 1)
                    zi = take(dve, j + 1)
                    link(dve.tensor_tensor(t, zi[:, :], sB, ALU.mult))
                    link(dve.tensor_tensor(yr, yr, t, ALU.subtract))
                    dve.tensor_tensor(t, zi[:, :], sD, ALU.mult).then_inc(ev_done, 1)
                    drained(dve, j + 1)
                    dve.tensor_tensor(yi, yi, t, ALU.add).then_inc(y_spec_ready, 1)
                    y = take(dve, j + 2)
                    dve.tensor_tensor(xn[:, g, 0:512], y[:, :], proj[:, g, 0:512], ALU.mult).then_inc(ev_done, 1)
                    drained(dve, j + 2)
                dve.sem_inc(hy_done, 1)

            def gla_gates():
                dve.wait_ge(gla_in, 64)
                dve.tensor_tensor(lbt, lb1, lb0, ALU.subtract).then_inc(lbd_ready, 1)
                dve.wait_ge(lb_ready, 2)
                for g in range(G):
                    pr = proj[:, g, :]
                    dve.wait_ge(sg3_ready, 4 * g + 4)
                    f = pr[:, CF:CF + 1024]
                    link(dve.tensor_tensor(pr[:, 0:1024], pr[:, 0:1024], lb1, ALU.mult))
                    link(dve.tensor_tensor(f, f, lb1, ALU.mult))
                    dve.tensor_tensor(f, f, lb0, ALU.add).then_inc(f_ready, 1)
                    q = pr[:, CQ:CQ + 512]
                    dve.tensor_tensor(q, q, lbt[:, 0:512] if g == 0 else wk[:, 3072:3584], ALU.mult).then_inc(q_ready, 1)
                    gg = pr[:, CG:CG + 512]
                    link(dve.tensor_tensor(gg, gg, pr[:, 1024:1536], ALU.mult))

            def gla(g):
                drained(dve, J[f"glaT{g}"] + 2)
                if g == 1:
                    dve.wait_ge(st_out, 32)
                dve.tensor_tensor(glaT[:, 3], glaT[:, 1], glaT[:, 2], ALU.add).then_inc(qk_ready, 1)

                def build(lev):
                    m = LEVELS[lev - 1]
                    if lev >= 3:
                        dve.wait_ge(mm_done, J[f"glaS{g}"] + lev - 2 + 1)

                    def par(v, k):
                        return v.rearrange("p h (b r m) -> p h b r m", r=2, m=m)[:, :, :, k, :]

                    Q = QK[:, lev % 2, 0, :].rearrange("p (h t) -> p h t", h=NHD)
                    K = QK[:, lev % 2, 1, :].rearrange("p (h t) -> p h t", h=NHD)
                    Ef, Eb = E[:, 0, :, lev - 1, :], E[:, 1, :, lev - 1, :]
                    for dst, src, e, k in ((Q, 0, Ef, 1), (Q, 0, Eb, 0), (K, 1, Ef, 0), (K, 2, Eb, 1)):
                        ins = dve.tensor_tensor(par(dst, k), par(glaT[:, src], k), par(e, k), ALU.mult)
                        if dst is K and k == 1:
                            ins.then_inc(qk_ready, 1)
                        else:
                            link(ins)

                def empty(lev):
                    bk = take(dve, J[f"glaS{g}"] + lev)
                    b4 = bk[:, :].rearrange("p (h t) -> p h t", h=NHD)
                    if lev == 0:
                        dve.tensor_tensor(accS, b4, ident.unsqueeze(1).to_broadcast([P, NHD, P]), ALU.mult).then_inc(ev_done, 1)
                    else:
                        mask = lmask[:, (lev - 1) * P:lev * P].unsqueeze(1).to_broadcast([P, NHD, P])
                        dve.copy_predicated(accS, mask, b4).then_inc(ev_done, 1)

                drained(dve, J[f"glaE{g}"] + 15)
                for lev in range(9):
                    if 1 <= lev < 8:
                        build(lev)
                    if lev >= 1:
                        empty(lev - 1)
                if g == 1:
                    dve.wait_ge(mm_done, J["glaS1"] + 8)
                    for r in range(2):
                        ins = dve.tensor_tensor(QK[:, 0, r, :].rearrange("p (h t) -> p h t", h=NHD), glaT[:, 0],
                                                E[:, r, :, 7, :], ALU.mult)
                        link(ins) if r == 0 else ins.then_inc(qc_ready, 1)
                bk = take(dve, J[f"glaO{g}"])
                dve.tensor_copy(ob, bk[:, :].rearrange("p (h t) -> p h t", h=NHD)).then_inc(ev_done, 1)
                drained(dve, J[f"glaO{g}"])
                if g == 0:
                    for r in range(2):
                        drained(dve, J["tailE"] + r)
                        kk = proj[:, g, r * 512:(r + 1) * 512]
                        dve.tensor_tensor(kk, kk, QK[:, 1, r, :], ALU.mult).then_inc(ko_ready, 1)
                sq = accS
                link(dve.tensor_tensor(sq, ob, ob, ALU.mult))
                ms = st[:, 16 + 4 * g:20 + 4 * g]
                link(dve.tensor_reduce(ms, sq, AX, ALU.add))
                dve.tensor_scalar(ms, ms, 1.0 / P, EPS, ALU.mult, ALU.add).then_inc(oss_ready, 1)
                dve.wait_ge(oms_ready, g + 1)
                rs = st[:, 8 + 4 * g:12 + 4 * g]
                link(dve.reciprocal(rs, rs))
                link(dve.tensor_tensor(ob, ob, rs.unsqueeze(2).to_broadcast([P, NHD, P]), ALU.mult))
                link(dve.tensor_tensor(ob, ob, nd[:, :].unsqueeze(1).to_broadcast([P, NHD, P]), ALU.mult))
                dve.tensor_tensor(xn[:, g, 512:1024].rearrange("p (h t) -> p h t", h=NHD), ob,
                                  proj[:, g, CG:CG + 512].rearrange("p (h t) -> p h t", h=NHD), ALU.mult).then_inc(o_ready, 1)

            dve.wait_ge(c_sig, 1)
            dve.wait_ge(c_ready, 1)
            for g in range(G):
                dve.tensor_tensor(cT[:, :, GROW * g], cvec[:, g, :], csg[:, g, :], ALU.mult).then_inc(c_ready, 1)
            for l in range(2):
                norm(4 * l)
                norm(4 * l + 1)
                ada(l)
                if l == 0:
                    link(dve.tensor_copy(lmask[:, :], proj[:, 0, 0:8 * P]))
                    bias_rows()
                if l == 0:
                    rope()
                    attention()
                else:
                    hyena()
                    gla_gates()
                    gla(0)
                    gla(1)
                add_out(l)
                norm(4 * l + 2)
                norm(4 * l + 3)
                top8(l)
                tokens(l)
                ranks()
                dense_hidden(sh_sg, l + 1, sh_step, l + 1, sh_h, SHB[l])
                positions(l)
                shared_out(l)
                experts(l)
            norm(8)
            norm(9)


_INS = ['x_prompt', 'x_sample', 'cache_a_k', 'cache_a_v', 'cache_b_k', 'cache_b_v', 'state_d_fwd', 'state_d_bwd', 'c',
        'c_ctx', 'w_ada', 'b_ada', 'norm_mix', 'norm_ffn', 'w_in_attn', 'w_out_attn', 'sink_a', 'rpb_b', 'w_in_rec',
        'w_out_rec', 'conv_w', 'conv_b', 'filt_w1', 'filt_b1', 'filt_w2', 'filt_b2', 'filt_w3', 'filt_b3', 'filt_freq',
        'filt_w4', 'd_skip', 'lb_fwd', 'lb_bwd', 'norm_d', 'w_router', 'router_bias', 'w_gate', 'w_up', 'w_down',
        'ws_gate', 'ws_up', 'ws_down', 'final_norm']
_OUTS = [("y_prompt", (1, 128, 1024)), ("y_sample", (1, 128, 1024)), ("new_a_k", (1, 1, 128, 2, 64)),
         ("new_a_v", (1, 1, 128, 2, 64)), ("new_b_k", (1, 1, 128, 8, 64)), ("new_b_v", (1, 1, 128, 8, 64)),
         ("new_d_fwd", (1, 1, 4, 128, 128)), ("new_d_bwd", (1, 1, 4, 128, 128))]


def kernel(**inputs):
    import numpy as _np
    import concourse.bacc as _bacc
    from concourse import mybir as _mybir
    from concourse.bass_utils import run_bass_kernel_spmd as _run

    nc = _bacc.Bacc("TRN2", target_bir_lowering=False, num_devices=1)
    place, cst, lmask = constants()
    arrays, args = {}, {}
    for name in _INS + ["cst", "lmask"]:
        a = cst if name == "cst" else lmask if name == "lmask" else _np.ascontiguousarray(inputs[name])
        arrays[f"in_{name}_dram"] = a
        args[name] = nc.dram_tensor(f"in_{name}_dram", a.shape, _mybir.dt.from_np(a.dtype), kind="ExternalInput").ap()
    outs = {}
    for name, shape in _OUTS:
        outs[name] = nc.dram_tensor(f"out_{name}_dram", shape, _mybir.dt.float32, kind="ExternalOutput").ap()
    trunk_kernel(nc, args, outs, place)
    r = _run(nc, [arrays], core_ids=[0])
    return tuple(r.results[0][f"out_{name}_dram"] for name, _ in _OUTS)
```
